# Optimizing a Trainium2 kernel written in Bass

```python
import jax, jax.numpy as jnp
from jax import lax
import numpy as np

D_MODEL = 2048
BATCH = 1
SEQ = 256
DEPTH = 1

POOL_WIDTH = D_MODEL // 2
POOL_WINDOWS = (2, 4, 8, 16)
N_POOL_GROUPS = len(POOL_WINDOWS)
POOL_GROUP = POOL_WIDTH // N_POOL_GROUPS
HEAD_DIM = 64
N_Q_HEADS = (D_MODEL - POOL_WIDTH) // HEAD_DIM
N_KV_HEADS = max(N_Q_HEADS // 4, 1)
Q_PER_KV = N_Q_HEADS // N_KV_HEADS
ATTN_WIDTH = N_Q_HEADS * HEAD_DIM
KV_WIDTH = N_KV_HEADS * HEAD_DIM
MIX_WIDTH = POOL_WIDTH + ATTN_WIDTH
IN_WIDTH = POOL_WIDTH + ATTN_WIDTH + 2 * KV_WIDTH
WINDOW = 128
BLOCK = 128
D_FF = (D_MODEL * 11) // 4
CONV_WIDTH = 3
EPS = 1e-6
NEG_INF = -1e30

kernel_name = "hybrid_pool_swa_alibi_convffn_encoder"

def rms_norm(x, g):
    xf = x.astype(jnp.float32)
    y = xf * lax.rsqrt(jnp.mean(xf * xf, axis=-1, keepdims=True) + EPS)
    return (y * g.astype(jnp.float32)).astype(x.dtype)

def alibi_slopes():
    i = np.arange(1, N_Q_HEADS + 1, dtype=np.float32)
    return jnp.asarray(np.power(2.0, -8.0 * i / N_Q_HEADS).astype(np.float32))

def pool_mixer(u, w_pool, pool_scale):
    b, s, _ = u.shape
    uf = u.astype(jnp.float32).reshape(b, s, N_POOL_GROUPS, POOL_GROUP)
    csum = jnp.pad(jnp.cumsum(uf, axis=1), ((0, 0), (1, 0), (0, 0), (0, 0)))
    t = jnp.arange(s)
    means = []
    for g, w in enumerate(POOL_WINDOWS):
        lo = jnp.clip(t - w // 2, 0, s)
        hi = jnp.clip(t + w // 2, 0, s)
        cnt = (hi - lo).astype(jnp.float32)
        c_g = csum[:, :, g]
        win = jnp.take(c_g, hi, axis=1) - jnp.take(c_g, lo, axis=1)
        means.append(win / cnt[None, :, None])
    mean = jnp.stack(means, axis=2)
    d = (mean - uf).astype(u.dtype)
    y = jnp.einsum('bsgc,gcd->bsgd', d, w_pool)
    return y.reshape(b, s, POOL_WIDTH) * pool_scale

def windowed_gqa(q, k, v, sink):
    b, s = q.shape[0], q.shape[1]
    nb = s // BLOCK
    qb = q.reshape(b, nb, BLOCK, N_KV_HEADS, Q_PER_KV, HEAD_DIM)
    qb = jnp.moveaxis(qb, 1, 0)
    pad = ((0, 0), (BLOCK, BLOCK), (0, 0), (0, 0))
    kp = jnp.pad(k, pad)
    vp = jnp.pad(v, pad)
    slopes = alibi_slopes().reshape(N_KV_HEADS, Q_PER_KV)
    sink_l = sink.astype(jnp.float32).reshape(N_KV_HEADS, Q_PER_KV)
    scale = HEAD_DIM ** -0.5

    def one_block(args):
        i, q_i = args
        k_i = lax.dynamic_slice_in_dim(kp, i * BLOCK, 3 * BLOCK, axis=1)
        v_i = lax.dynamic_slice_in_dim(vp, i * BLOCK, 3 * BLOCK, axis=1)
        qpos = i * BLOCK + jnp.arange(BLOCK)
        kpos = i * BLOCK - BLOCK + jnp.arange(3 * BLOCK)
        dist = jnp.abs(qpos[:, None] - kpos[None, :])
        valid = (dist <= WINDOW) & (kpos >= 0)[None, :] & (kpos < s)[None, :]
        logits = jnp.einsum('bqhgd,bkhd->bhgqk', q_i, k_i,
                            preferred_element_type=jnp.float32) * scale
        logits = logits - slopes[None, :, :, None, None] * dist.astype(jnp.float32)
        logits = jnp.where(valid, logits, NEG_INF)
        sink_col = jnp.broadcast_to(sink_l[None, :, :, None, None], logits.shape[:-1] + (1,))
        probs = jax.nn.softmax(jnp.concatenate([logits, sink_col], axis=-1), axis=-1)[..., :-1]
        out = jnp.einsum('bhgqk,bkhd->bqhgd', probs.astype(v.dtype), v_i)
        return out.reshape(b, BLOCK, ATTN_WIDTH)

    outs = lax.map(one_block, (jnp.arange(nb), qb))
    return jnp.moveaxis(outs, 0, 1).reshape(b, s, ATTN_WIDTH)

def conv_ffn(h, w_gate, w_up, conv_w, conv_b, w_down):
    gate = h @ w_gate
    up = h @ w_up
    gp = jnp.pad(gate, ((0, 0), (1, 1), (0, 0)))
    gate = gp[:, :-2] * conv_w[0] + gp[:, 1:-1] * conv_w[1] + gp[:, 2:] * conv_w[2] + conv_b
    return (jax.nn.gelu(gate, approximate=True) * up) @ w_down

def setup_inputs(seed: int = 0) -> dict:
    key = jax.random.key(seed)
    ks = jax.random.split(key, 16)
    f32 = jnp.float32
    L = DEPTH

    def nrm(k, shape, scale):
        return jax.random.normal(k, shape, f32) * scale

    return {
        "x": jax.random.normal(ks[0], (BATCH, SEQ, D_MODEL), f32),
        "norm_pre_mix": 1.0 + nrm(ks[1], (L, D_MODEL), 0.05),
        "w_in": nrm(ks[2], (L, D_MODEL, IN_WIDTH), D_MODEL ** -0.5),
        "w_pool": nrm(ks[3], (L, N_POOL_GROUPS, POOL_GROUP, POOL_GROUP), POOL_GROUP ** -0.5),
        "pool_scale": 1.0 + nrm(ks[4], (L, POOL_WIDTH), 0.1),
        "attn_sink": nrm(ks[5], (L, N_Q_HEADS), 0.5),
        "w_out": nrm(ks[6], (L, MIX_WIDTH, D_MODEL), MIX_WIDTH ** -0.5),
        "norm_post_mix": 1.0 + nrm(ks[7], (L, D_MODEL), 0.05),
        "norm_pre_ffn": 1.0 + nrm(ks[8], (L, D_MODEL), 0.05),
        "w_gate": nrm(ks[9], (L, D_MODEL, D_FF), D_MODEL ** -0.5),
        "w_up": nrm(ks[10], (L, D_MODEL, D_FF), D_MODEL ** -0.5),
        "conv_w": nrm(ks[11], (L, CONV_WIDTH, D_FF), CONV_WIDTH ** -0.5),
        "conv_b": nrm(ks[12], (L, D_FF), 0.01),
        "w_down": nrm(ks[13], (L, D_FF, D_MODEL), D_FF ** -0.5),
        "norm_post_ffn": 1.0 + nrm(ks[14], (L, D_MODEL), 0.05),
    }

def reference(x, norm_pre_mix, w_in, w_pool, pool_scale, attn_sink, w_out, norm_post_mix,
              norm_pre_ffn, w_gate, w_up, conv_w, conv_b, w_down, norm_post_ffn):
    b, s, _ = x.shape
    for l in range(DEPTH):
        h = rms_norm(x, norm_pre_mix[l])
        p = h @ w_in[l]
        o0 = POOL_WIDTH
        o1 = o0 + ATTN_WIDTH
        o2 = o1 + KV_WIDTH
        u_pool = p[..., :o0]
        q = p[..., o0:o1].reshape(b, s, N_Q_HEADS, HEAD_DIM)
        k = p[..., o1:o2].reshape(b, s, N_KV_HEADS, HEAD_DIM)
        v = p[..., o2:].reshape(b, s, N_KV_HEADS, HEAD_DIM)
        y_pool = pool_mixer(u_pool, w_pool[l], pool_scale[l])
        y_attn = windowed_gqa(q, k, v, attn_sink[l])
        mix = jnp.concatenate([y_pool, y_attn], axis=-1) @ w_out[l]
        x = x + rms_norm(mix, norm_post_mix[l])
        f = rms_norm(x, norm_pre_ffn[l])
        y = conv_ffn(f, w_gate[l], w_up[l], conv_w[l], conv_b[l], w_down[l])
        x = x + rms_norm(y, norm_post_ffn[l])
    return x


_drawn_inputs = setup_inputs


def setup_inputs(seed=0):
    import zlib

    import numpy as np

    out = dict(_drawn_inputs(seed))
    spreads = {}
    factors = {'attn_sink': 6.867, 'conv_b': 8.0}
    for name, (base, spread) in spreads.items():
        noise = np.random.default_rng([zlib.crc32(name.encode()), seed]).standard_normal(out[name].shape)
        drawn = base * np.exp(spread * noise) if base else spread * noise
        out[name] = __import__('jax').numpy.asarray(drawn.astype(out[name].dtype))
    for name, factor in factors.items():
        out[name] = (out[name] * factor).astype(out[name].dtype)
    return out
```

```python
from contextlib import ExitStack

import numpy as np
import concourse.bass as bass
from concourse import mybir

F32 = mybir.dt.float32
F32R = mybir.dt.float32r
ALU = mybir.AluOpType
ACT = mybir.ActivationFunctionType
AX_X = mybir.AxisListType.X

P = 128
D = 2048
S = 256
TB = S // P
KT = D // P
POOL_W = D // 2
WINDOWS = (2, 4, 8, 16)
HD = 64
NQ = (D - POOL_W) // HD
NKV = NQ // 4
KV_W = NKV * HD
IN_W = POOL_W + NQ * HD + 2 * KV_W
WINDOW = 128
FF = D * 11 // 4
FT = FF // P
EPS = 1e-6
FAR = 1e33

RING = 4
U_Q, U_POOL, U_OUT = 4, 12, 20
U_FFN = U_OUT + KT
U_DOWN = U_FFN + 2 * FT
UNITS = U_DOWN + FT
PAD = max(WINDOWS) // 2
PW = S + 2 * PAD
REACH = {1: 7, 2: 6, 4: 4, 8: 0}
SLOPES = [float(np.float32(2.0) ** np.float32(-8.0 * (h + 1) / NQ)) for h in range(NQ)]

MIX = 0
Q0, D0, WP0, K0 = 16, 24, 32, 40


def layer(nc, x, norm_pre_mix, w_in, w_pool, pool_scale, attn_sink, w_out, norm_post_mix,
          norm_pre_ffn, w_gate, w_up, conv_w, conv_b, w_down, norm_post_ffn,
          identity, distance, inverse_count, out):
    x_rows = x.rearrange("a (b p) d -> (a b) p d", p=P)
    out_rows = out.rearrange("a (b p) d -> (a b) p d", p=P)
    w_in_v = w_in.rearrange("l (k p) n -> p (l k) n", p=P)
    w_gate_v = w_gate.rearrange("l (k p) n -> p (l k) n", p=P)
    w_up_v = w_up.rearrange("l (k p) n -> p (l k) n", p=P)
    w_out_v = w_out.rearrange("l (k p) n -> p (l k) n", p=P)
    w_down_v = w_down.rearrange("l (k p) n -> p (l k) n", p=P)
    w_pool_v = w_pool.rearrange("l g (c p) d -> p (l g c) d", p=P)

    with ExitStack() as ctx:
        def sb(name, shape, dt=F32):
            return ctx.enter_context(nc.sbuf_tensor(name, shape, dt))

        def sem(name):
            return ctx.enter_context(nc.semaphore(name))

        raw = sb("raw", [P, RING, D])
        hi = sb("hi", [P, RING, D], F32R)
        lo = sb("lo", [P, RING, D], F32R)
        act = sb("act", [P, KT, 2 * S], F32R)
        pair = sb("pair", [P, RING, 2 * S], F32R)
        xbuf = sb("xbuf", [P, TB, D])
        late = sb("late", [P, FT, S])
        pads = sb("pads", [P, 4, PW])
        half = sb("half", [P, 2, S])
        dist = sb("dist", [P, TB, S])
        ident = sb("ident", [P, P])
        rows_a = sb("rows_a", [P, P])
        rows_b = sb("rows_b", [P, P])
        cols = sb("cols", [P, 4 * FT + 8])
        sink = sb("sink", [P, NQ])
        neg_sink = sb("neg_sink", [P, NQ])
        stat = sb("stat", [P, 8])
        expo = sb("expo", [P, 1])
        small = sb("small", [P, 2, 6, 4])
        psum = ctx.enter_context(nc.psum_tensor("psum", [P, 8, 512], F32))

        xflat = xbuf[:, :, :].rearrange("p b d -> p (b d)")
        prob = [xflat[:, 1024 * b:1024 * (b + 1)].rearrange("p (h s) -> p h s", h=4) for b in range(2)]
        prob_t = xflat[:, 2048:3072].rearrange("p (k c) -> p k c", k=2)
        val = xflat[:, 3072:3584].rearrange("p (b c) -> p b c", b=2)
        val_t = xflat[:, 3584:4096].rearrange("p (u s) -> p u s", u=2)
        wide = lambda a, n=8: late[:, a:a + n, :].rearrange("p t s -> p (t s)")
        inv_count = late[:, MIX:MIX + 4, :]
        CW0, CW1, PS, CW2, CB = 0, FT, 2 * FT, 2 * FT + 8, 3 * FT + 8

        raw_landed = [sem(f"raw_landed_{s}") for s in range(RING)]
        x_landed = [sem(f"x_landed_{b}") for b in range(TB)]
        gain_landed = sem("gain_landed")
        const_landed = sem("const_landed")
        rows_landed = sem("rows_landed")
        pool_const_landed = sem("pool_const_landed")
        x_again_landed = sem("x_again_landed")
        gains2_landed = sem("gains2_landed")
        gain3_landed = sem("gain3_landed")
        stored = sem("stored")
        hi_ready = sem("hi_ready")
        lo_ready = sem("lo_ready")
        unit_done = sem("unit_done")
        pair_hi = sem("pair_hi")
        pair_lo = sem("pair_lo")
        half_ready = sem("half_ready")
        result_ready = sem("result_ready")
        squares = sem("squares")
        rms_ready = sem("rms_ready")
        rms_step = sem("rms_step")
        exp_set = sem("exp_set")
        normed = sem("normed")
        turned = sem("turned")
        act_hi = sem("act_hi")
        act_lo = sem("act_lo")
        params_turned = sem("params_turned")
        params_ready = sem("params_ready")
        val_turned = sem("val_turned")
        val_ready = sem("val_ready")
        sink_ready = sem("sink_ready")
        pads_zero = sem("pads_zero")
        scores_done = sem("scores_done")
        logits_ready = sem("logits_ready")
        max_step = sem("max_step")
        bias_ready = sem("bias_ready")
        exps_ready = sem("exps_ready")
        sum_step = sem("sum_step")
        prob_ready = sem("prob_ready")
        prob_turned = sem("prob_turned")
        prob_t_ready = sem("prob_t_ready")
        heads_done = sem("heads_done")
        heads_ready = sem("heads_ready")
        pool_step = sem("pool_step")
        diff_ready = sem("diff_ready")
        pooled = sem("pooled")
        pooled_ready = sem("pooled_ready")
        resid = sem("resid")
        conv_step = sem("conv_step")
        conv_ready = sem("conv_ready")
        gelu_ready = sem("gelu_ready")
        hidden_ready = sem("hidden_ready")

        block = ctx.enter_context(nc.Block())

        @block.sync
        def _(sp):
            def load(n, c, src):
                if not isinstance(n, int) or n >= RING:
                    sp.wait_ge(lo_ready, n - RING + 1)
                dst = raw[:, c, :]
                if len(src.shape) == 3:
                    dst = dst.rearrange("p (k n) -> p k n", k=KT)
                sp.dma_start(dst, src).then_inc(raw_landed[c], 16)

            def in_columns(first):
                return w_in_v[:, :, first:first + P]

            for b in range(TB):
                sp.dma_start(xbuf[:, b, :], x_rows[b]).then_inc(x_landed[b], 16)
            sp.dma_start(wide(WP0), norm_pre_mix.partition_broadcast(P).rearrange("p l d -> p (l d)")).then_inc(gain_landed, 16)
            for c, first in enumerate((IN_W - 2 * KV_W, IN_W - 2 * KV_W + P, IN_W - KV_W, IN_W - KV_W + P)):
                load(c, c, in_columns(first))
            with sp.Fori(0, 2) as i:
                for c in range(RING):
                    load(i * RING + (U_Q + c), c, w_in_v[:, :, bass.ds(i * (RING * P) + (POOL_W + c * P), P)])
            sp.wait_ge(normed, TB)
            sp.dma_start(late[:, WP0:WP0 + 8, :], w_pool_v).then_inc(pool_const_landed, 16)
            for m in range(8):
                load(U_POOL + m, m % RING, in_columns((7 - m) * P))
            for r in range(KT):
                if r == 6:
                    sp.wait_ge(heads_done, 8)
                    sp.wait_ge(heads_ready, 8)
                    for b in range(TB):
                        sp.dma_start(xbuf[:, b, :], x_rows[b]).then_inc(x_again_landed, 16)
                    sp.wait_ge(pooled, 4)
                    for a, g in ((Q0, norm_post_mix), (D0, norm_pre_ffn)):
                        sp.dma_start(wide(a), g.partition_broadcast(P).rearrange("p l d -> p (l d)")).then_inc(gains2_landed, 16)
                load(U_OUT + r, r % RING, w_out_v[:, (r + 8) % KT, :])
            with sp.Fori(0, FT // 2) as i:
                for c in range(RING):
                    w = (w_gate_v, w_up_v)[c % 2]
                    load(i * RING + (U_FFN + c), c, w[:, :, bass.ds(i * (2 * P) + (c // 2) * P, P)])
            with sp.Fori(0, FT // RING) as i:
                for c in range(RING):
                    load(i * RING + (U_DOWN + c), c, w_down_v[:, i * RING + c, :])
            sp.wait_ge(pair_lo, KT + FT)
            sp.dma_start(wide(0), norm_post_ffn.partition_broadcast(P).rearrange("p l d -> p (l d)")).then_inc(gain3_landed, 16)
            for b in range(TB):
                sp.wait_ge(resid, 2 * TB + 2 * (b + 1))
                sp.dma_start(out_rows[b], xbuf[:, b, :]).then_inc(stored, 16)
            sp.wait_ge(stored, 16 * TB)

        @block.tensor
        def _(pe):
            def turn(first_block, source, count):
                for b in range(TB):
                    pe.wait_ge(normed, first_block + b + 1)
                    for kt in range(KT):
                        mm = nc.tensor.transpose(psum[:, kt // 2, (kt % 2) * S + b * P:(kt % 2) * S + b * P + P],
                                                 source[b][:, kt * P:(kt + 1) * P], ident[:, :])
                    mm.then_inc(turned, 1)

            def column_unit(n, c, bank, free_after, first_norm):
                pe.wait_ge(lo_ready, n + 1)
                if first_norm is not None:
                    pe.wait_ge(act_lo, first_norm)
                if free_after is not None:
                    pe.wait_ge(result_ready, free_after)
                for kt in range(KT):
                    high = (hi[:, c, kt * P:(kt + 1) * P], act[:, kt, :], psum[:, bank, :])
                    low = (lo[:, c, kt * P:(kt + 1) * P], act[:, kt, 0:S], psum[:, bank, 0:S])
                    last = kt == KT - 1
                    for k, (w, a, o) in enumerate((low, high) if last else (high, low)):
                        mm = nc.tensor.matmul(o, w, a, start=(kt == 0 and k == 0), stop=(last and k == 1))
                mm.then_inc(unit_done, 1)

            def row_unit(n, c, pairs, start, stop, banks):
                pe.wait_ge(lo_ready, n + 1)
                pe.wait_ge(pair_lo, pairs)
                for b in range(TB):
                    for j in range(4):
                        o = psum[:, banks[b] + j, :]
                        a_hi = pair[:, c, b * P:(b + 1) * P]
                        a_lo = pair[:, c, S + b * P:S + (b + 1) * P]
                        w_hi = hi[:, c, j * 512:(j + 1) * 512]
                        w_lo = lo[:, c, j * 512:(j + 1) * 512]
                        nc.tensor.matmul(o, a_hi, w_hi, start=start, stop=False)
                        nc.tensor.matmul(o, a_hi, w_lo, start=False, stop=False)
                        mm = nc.tensor.matmul(o, a_lo, w_hi, start=False, stop=stop)
                mm.then_inc(unit_done, 1)

            def scores(m):
                if m >= 1:
                    pe.wait_ge(logits_ready, m)
                j, qb = m // 2, m % 2
                for e in range(2):
                    for t in range(2):
                        r = slice(64 * e, 64 * e + 64)
                        mm = nc.tensor.matmul(psum[:, 4 + e, t * S:(t + 1) * S],
                                              late[r, Q0 + 2 * j + t, qb * P:(qb + 1) * P],
                                              late[r, K0 + j, :], start=True, stop=True)
                mm.then_inc(scores_done, 1)

            def turn_probs(m):
                pe.wait_ge(prob_ready, m + 1)
                if m >= 1:
                    pe.wait_ge(prob_t_ready, m)
                for kb in range(2):
                    for hh in range(4):
                        mm = nc.tensor.transpose(psum[:, 6 + kb, hh * P:(hh + 1) * P],
                                                 prob[m % 2][:, hh, kb * P:(kb + 1) * P], ident[:, :])
                mm.then_inc(prob_turned, 1)

            def heads(m):
                pe.wait_ge(prob_t_ready, m + 1)
                if m >= 2:
                    pe.wait_ge(heads_ready, m - 1)
                j = m // 2
                for e in range(2):
                    for kb in range(2):
                        rhs = prob_t[:, kb, :].rearrange("p (t e q) -> p t e q", t=2, e=2)[:, :, e, :]
                        mm = nc.tensor.matmul(psum[64 * e:64 * e + 64, 2 + m % 2, 0:S],
                                              val[:, kb, j * HD:(j + 1) * HD], rhs,
                                              start=(kb == 0), stop=(kb == 1))
                mm.then_inc(heads_done, 1)

            pe.wait_ge(const_landed, 32)
            pe.wait_ge(rows_landed, 16 * 5)
            nc.tensor.transpose(psum[:, 0, 0:2 * FT + 8], rows_a[0:2 * FT + 8, :], ident[0:2 * FT + 8, 0:2 * FT + 8])
            nc.tensor.transpose(psum[:, 0, 2 * FT + 8:4 * FT + 8], rows_b[0:2 * FT, :],
                                ident[0:2 * FT, 0:2 * FT]).then_inc(params_turned, 1)
            pe.wait_ge(params_ready, 1)
            turn(0, [xbuf[:, b, :] for b in range(TB)], 0)

            for n in range(U_Q):
                column_unit(n, n, n % 2, n - 1 if n >= 2 else None, 8)
            with pe.Fori(0, 2) as i:
                for c in range(RING):
                    column_unit(i * RING + (U_Q + c), c, c % 2, i * RING + (U_Q + c - 1), None)
            pe.wait_ge(result_ready, U_Q)
            for tb in range(TB):
                for u in range(2):
                    mm = nc.tensor.transpose(psum[:, 6, (tb * 2 + u) * P:(tb * 2 + u + 1) * P],
                                             val_t[:, u, tb * P:(tb + 1) * P], ident[:, :])
            mm.then_inc(val_turned, 1)
            for m in range(8):
                if m == 0:
                    pe.wait_ge(result_ready, U_POOL)
                scores(m)
                n = U_POOL + m
                column_unit(n, n % RING, n % 2, n - 1, None)
                if m >= 2:
                    heads(m - 2)
                if m == 1:
                    pe.wait_ge(val_ready, 1)
                if m >= 1:
                    turn_probs(m - 1)
            heads(6)
            turn_probs(7)
            pe.wait_ge(pool_const_landed, 16)
            for k, g in enumerate((3, 2, 1, 0)):
                pe.wait_ge(diff_ready, 2 * k + 2)
                if k == 0:
                    pe.wait_ge(result_ready, U_OUT)
                    pe.wait_ge(logits_ready, 8)
                for mt in range(2):
                    for kc in range(2):
                        mm = nc.tensor.matmul(psum[:, (0, 1, 4, 5)[g], mt * S:(mt + 1) * S],
                                              late[:, WP0 + 2 * g + kc, mt * P:(mt + 1) * P],
                                              late[:, D0 + 2 * g + kc, :], start=(kc == 0), stop=(kc == 1))
                mm.then_inc(pooled, 1)
            heads(7)

            pe.wait_ge(pooled_ready, 8)
            pe.wait_ge(heads_ready, 8)
            for r in range(KT):
                row_unit(U_OUT + r, r % RING, r + 1, r == 0, r == KT - 1, (0, 4))

            pe.wait_ge(resid, 2 * TB - 1)
            turn(TB, [wide(WP0), wide(MIX)], 1)

            for c in range(RING):
                column_unit(U_FFN + c, c, c, None, 16)
            with pe.Fori(1, FT // 2) as i:
                for c in range(RING):
                    column_unit(i * RING + (U_FFN + c), c, c, i * RING + (U_OUT + c - RING + 1), None)

            pe.wait_ge(result_ready, U_OUT + 2 * FT)
            for c in range(RING):
                row_unit(U_DOWN + c, c, KT + c + 1, c == 0, False, (4, 0))
            with pe.Fori(1, FT // RING - 1) as i:
                for c in range(RING):
                    row_unit(i * RING + (U_DOWN + c), c, i * RING + (KT + c + 1), False, False, (4, 0))
            for c in range(RING):
                n = UNITS - RING + c
                row_unit(n, c, KT + FT - RING + c + 1, False, c == RING - 1, (4, 0))

        @block.scalar
        def _(sc):
            def split(n, c):
                sc.wait_ge(raw_landed[c], (n // RING) * 16 + 16 if isinstance(n, int) else n)
                nc.scalar.copy(hi[:, c, :], raw[:, c, :]).then_inc(hi_ready, 1)

            def split_unit(n, c):
                if n >= RING:
                    sc.wait_ge(unit_done, n - RING + 1)
                split(n, c)

            def split_looped(i, first, c):
                sc.wait_ge(unit_done, i * RING + (first + c - RING + 1))
                sc.wait_ge(raw_landed[c], i * 16 + (first // RING + 1) * 16)
                nc.scalar.copy(hi[:, c, :], raw[:, c, :]).then_inc(hi_ready, 1)

            def split_pair(tile, c):
                nc.scalar.copy(pair[:, c, 0:S], late[:, tile, :]).then_inc(pair_hi, 1)

            def half_out(n, bank, scale=1.0):
                sc.wait_ge(unit_done, n + 1)
                nc.scalar.activation(half[:, bank % 2, :], psum[:, bank, S:2 * S], ACT.Copy, scale=scale).then_inc(half_ready, 1)

            def act_high(first):
                for k in range(8):
                    if k == 0:
                        sc.wait_ge(turned, first)
                    nc.scalar.copy(act[:, 2 * k:2 * k + 2, 0:S], psum[:, k, :].rearrange("p (t s) -> p t s", t=2)).then_inc(act_hi, 1)

            def square(source, k):
                if k:
                    sc.wait_ge(squares, k)
                nc.scalar.activation(wide(MIX + 8), source, ACT.Square, accum_out=stat[:, k:k + 1]).then_inc(squares, 1)

            sc.dma_start(ident[:, :], identity).then_inc(const_landed, 16)
            sc.dma_start(dist[:, :, :], distance.rearrange("b p s -> p b s")).then_inc(const_landed, 16)
            for k, (dst, a, src) in enumerate(((rows_a, 0, conv_w[0, 0]), (rows_a, FT, conv_w[0, 1]), (rows_a, 2 * FT, pool_scale[0]),
                                               (rows_b, 0, conv_w[0, 2]), (rows_b, FT, conv_b[0]))):
                t = src.shape[0] // P
                sc.dma_start(dst[a:a + t, :], src.rearrange("(t p) -> t p", p=P)).then_inc(rows_landed, 16)
            sc.dma_start(sink[:, :], attn_sink.partition_broadcast(P).rearrange("p l h -> p (l h)")).then_inc(pool_const_landed, 16)
            sc.dma_start(inv_count, inverse_count.partition_broadcast(P)).then_inc(pool_const_landed, 16)
            for b in range(TB):
                sc.wait_ge(x_landed[b], 16)
                square(xbuf[:, b, :], b)
            for c in range(RING):
                split_unit(c, c)
            act_high(TB)

            for n in range(U_Q):
                if n >= 2:
                    sc.wait_ge(result_ready, n - 1)
                half_out(n, n % 2)
                split_unit(n + RING, n % RING)
            with sc.Fori(0, 2) as i:
                for c in range(RING):
                    sc.wait_ge(result_ready, i * RING + (U_Q + c - 1))
                    half_out(i * RING + (U_Q + c), c % 2, HD ** -0.5)
                    split_looped(i, 2 * RING, c)
            sc.wait_ge(val_turned, 1)
            nc.scalar.copy(val, psum[:, 6, :].rearrange("p (b c) -> p b c", b=2)).then_inc(val_ready, 1)

            def exps(m):
                sc.wait_ge(bias_ready, m + 1)
                s = small[:, m % 2]
                for hh in range(4):
                    h = prob[m % 2][:, hh, :]
                    nc.scalar.activation(h, h, ACT.Exp, bias=s[:, 1, hh:hh + 1], accum_out=s[:, 3, hh:hh + 1])
                nc.scalar.activation(s[:, 4, :], s[:, 2, :], ACT.Exp).then_inc(exps_ready, 1)

            def probs_out(m):
                sc.wait_ge(prob_turned, m + 1)
                if m >= 1:
                    sc.wait_ge(heads_done, m)
                nc.scalar.copy(prob_t, psum[:, 6:8, :]).then_inc(prob_t_ready, 1)

            def heads_out(m):
                sc.wait_ge(heads_done, m + 1)
                j, qb = m // 2, m % 2
                nc.scalar.copy(late[:, MIX + 8 + 2 * j:MIX + 10 + 2 * j, qb * P:(qb + 1) * P],
                               psum[:, 2 + m % 2, 0:S].rearrange("p (t q) -> p t q", t=2)).then_inc(heads_ready, 1)

            for m in range(8):
                n = U_POOL + m
                exps(m)
                sc.wait_ge(result_ready, n - 1)
                half_out(n, n % 2)
                if m >= 2:
                    heads_out(m - 2)
                if m >= 1:
                    probs_out(m - 1)
                split_unit(n + RING, n % RING)
                if m >= RING:
                    r = m - RING
                    sc.wait_ge(heads_ready, 2 * (r // 2) + 2)
                    split_pair(MIX + 8 + r, r)
            heads_out(6)
            probs_out(7)
            for k, g in enumerate((3, 2, 1, 0)):
                sc.wait_ge(pooled, k + 1)
                if k == 0:
                    sc.wait_ge(params_ready, 1)
                    sc.wait_ge(diff_ready, 8)
                for mt in range(2):
                    t = 2 * g + mt
                    nc.scalar.activation(late[:, MIX + t, :], psum[:, (0, 1, 4, 5)[g], mt * S:(mt + 1) * S], ACT.Copy,
                                         scale=cols[:, PS + t:PS + t + 1]).then_inc(pooled_ready, 1)
            heads_out(7)

            for r in range(KT):
                n = U_OUT + r
                split_unit(n + RING, r % RING)
                if r + RING < KT:
                    if r == 0:
                        sc.wait_ge(heads_ready, 8)
                        sc.wait_ge(pooled_ready, 8)
                    split_pair(MIX + (r + RING + 8) % KT, r % RING)

            for b in range(TB):
                if b == 0:
                    sc.wait_ge(unit_done, U_FFN)
                    sc.wait_ge(pair_lo, KT)
                square(psum[:, 4 * b:4 * b + 4, :].rearrange("p b c -> p (b c)"), 2 + b)
            for b in range(TB):
                sc.wait_ge(resid, 2 * b + 2)
                square(xbuf[:, b, :], 4 + b)
            act_high(2 * TB)

            def ffn_tile(i, ct, first):
                for k in range(2):
                    c = 2 * ct + k
                    if not (first and ct == 0):
                        sc.wait_ge(result_ready, i * RING + (U_OUT + c - 1))
                    half_out(i * RING + (U_FFN + c), c)
                    if k == 0:
                        sc.wait_ge(conv_ready, i * 2 + (ct + 1))
                        nc.scalar.activation(half_gelu, half_gelu, ACT.Gelu_apprx_tanh,
                                             bias=cols[:, bass.ds(i * 2 + (CB + ct), 1)]).then_inc(gelu_ready, 1)
                    split_looped(i, U_FFN + RING, c)

            half_gelu = pads[:, 1, 0:S]
            with sc.Fori(0, FT // 2 - 1) as i:
                for ct in range(2):
                    ffn_tile(i, ct, False)
            i = FT // 2 - 1
            for ct in range(2):
                ffn_tile(i, ct, False)
                for k in range(2):
                    c = 2 * ct + k
                    sc.wait_ge(hidden_ready, c + 1)
                    split_pair(c, c)

            with sc.Fori(0, FT // RING - 1) as i:
                for c in range(RING):
                    split_looped(i, U_DOWN + RING, c)
                    split_pair(i * RING + (RING + c), c)

            for b in range(TB):
                if b == 0:
                    sc.wait_ge(unit_done, UNITS)
                    sc.wait_ge(pair_lo, KT + FT)
                square(psum[:, 4 - 4 * b:8 - 4 * b, :].rearrange("p b c -> p (b c)"), 6 + b)

        @block.vector
        def _(ve):
            def split(n, c):
                ve.wait_ge(hi_ready, n + 1)
                nc.vector.tensor_tensor(lo[:, c, :], raw[:, c, :], hi[:, c, :].bitcast(F32), ALU.subtract).then_inc(lo_ready, 1)

            def split_pair(tile, c, count):
                ve.wait_ge(pair_hi, count)
                nc.vector.tensor_tensor(pair[:, c, S:2 * S], late[:, tile, :], pair[:, c, 0:S].bitcast(F32),
                                        ALU.subtract).then_inc(pair_lo, 1)

            def act_low(first):
                for k in range(8):
                    ve.wait_ge(act_hi, first + k + 1)
                    nc.vector.tensor_tensor(act[:, 2 * k:2 * k + 2, S:2 * S], psum[:, k, :].rearrange("p (t s) -> p t s", t=2),
                                            act[:, 2 * k:2 * k + 2, 0:S].bitcast(F32), ALU.subtract).then_inc(act_lo, 1)

            nc.vector.memset(pads[:, :, :], 0.0).then_inc(pads_zero, 1)
            nc.vector.memset(expo[:, :], -0.5).then_inc(exp_set, 1)
            ve.wait_ge(params_turned, 1)
            nc.vector.tensor_copy(cols[:, :], psum[:, 0, 0:4 * FT + 8]).then_inc(params_ready, 1)
            ve.wait_ge(pool_const_landed, 32)
            nc.vector.tensor_scalar(neg_sink[:, :], sink[:, :], -1.0, None, ALU.mult).then_inc(sink_ready, 1)
            ve.wait_ge(gain_landed, 16)
            for b in range(TB):
                ve.wait_ge(rms_ready, b + 1)
                nc.vector.scalar_tensor_tensor(out=xbuf[:, b, :], in0=xbuf[:, b, :], scalar=stat[:, b:b + 1], in1=wide(WP0),
                                               op0=ALU.mult, op1=ALU.mult).then_inc(normed, 1)
            for c in range(RING):
                split(c, c)
            act_low(0)

            for n in range(2):
                ve.wait_ge(half_ready, n + 1)
                for e in range(2):
                    for to in range(2):
                        s, r = slice(64 * e, 64 * e + 64), slice(64 * to, 64 * to + 64)
                        op = nc.vector.tensor_tensor(late[r, K0 + 2 * n + e, :], psum[s, n, 0:S], half[s, n, :], ALU.add)
                op.then_inc(result_ready, 1)
                split(n + RING, n)
            for n in range(2, 4):
                ve.wait_ge(half_ready, n + 1)
                nc.vector.tensor_tensor(val_t[:, n - 2, :], psum[:, n % 2, 0:S], half[:, n % 2, :], ALU.add).then_inc(result_ready, 1)
                split(n + RING, n)
            with ve.Fori(0, 2) as i:
                for c in range(RING):
                    ve.wait_ge(half_ready, i * RING + (U_Q + c + 1))
                    nc.vector.scalar_tensor_tensor(out=late[:, i * RING + (Q0 + c), :], in0=psum[:, c % 2, 0:S], scalar=HD ** -0.5,
                                                   in1=half[:, c % 2, :], op0=ALU.mult, op1=ALU.add).then_inc(result_ready, 1)
                    split(i * RING + (2 * RING + c), c)

            ve.wait_ge(sink_ready, 1)
            ve.wait_ge(const_landed, 32)
            for m in range(8):
                n, j, qb = U_POOL + m, m // 2, m % 2
                s, p = small[:, m % 2], prob[m % 2]
                ve.wait_ge(scores_done, m + 1)
                if m >= 2:
                    ve.wait_ge(prob_turned, m - 1)
                for hh in range(4):
                    op = nc.vector.scalar_tensor_tensor(out=p[:, hh, :], in0=dist[:, qb, :], scalar=-SLOPES[4 * j + hh],
                                                        in1=psum[:, 4 + hh % 2, (hh // 2) * S:(hh // 2 + 1) * S],
                                                        op0=ALU.mult, op1=ALU.add)
                op.then_inc(logits_ready, 1)
                ve.wait_ge(logits_ready, m + 1)
                nc.vector.reduce_max(s[:, 0, :], p, AX_X).then_inc(max_step, 1)
                ve.wait_ge(max_step, 2 * m + 1)
                nc.vector.scalar_tensor_tensor(out=s[:, 1, :], in0=s[:, 0, :], scalar=-1.0, in1=neg_sink[:, 4 * j:4 * j + 4],
                                               op0=ALU.mult, op1=ALU.min).then_inc(max_step, 1)
                ve.wait_ge(max_step, 2 * m + 2)
                nc.vector.tensor_tensor(s[:, 2, :], s[:, 1, :], sink[:, 4 * j:4 * j + 4], ALU.add).then_inc(bias_ready, 1)
                if m >= 1:
                    split(n + RING - 1, (n - 1) % RING)
                ve.wait_ge(exps_ready, m + 1)
                nc.vector.tensor_tensor(s[:, 3, :], s[:, 3, :], s[:, 4, :], ALU.add).then_inc(sum_step, 1)
                ve.wait_ge(sum_step, 2 * m + 1)
                nc.vector.reciprocal(s[:, 5, :], s[:, 3, :]).then_inc(sum_step, 1)
                ve.wait_ge(sum_step, 2 * m + 2)
                for hh in range(4):
                    op = nc.vector.tensor_scalar(p[:, hh, :], p[:, hh, :], s[:, 5, hh:hh + 1], None, ALU.mult)
                op.then_inc(prob_ready, 1)
                ve.wait_ge(half_ready, n + 1)
                if m >= 2:
                    ve.wait_ge(diff_ready, m - 1)
                nc.vector.tensor_tensor(pads[:, m % 2, PAD:PAD + S], psum[:, n % 2, 0:S], half[:, n % 2, :],
                                        ALU.add).then_inc(result_ready, 1)
                if m >= RING:
                    split_pair(MIX + 8 + m - RING, m - RING, m - RING + 1)
            split(U_OUT + RING - 1, RING - 1)

            for r in range(KT):
                split(U_OUT + r + RING, r % RING)
                if r + RING < KT:
                    split_pair(MIX + (r + RING + 8) % KT, r % RING, r + RING + 1)

            def residual(b, banks, norm, gain, temp, count):
                ve.wait_ge(rms_ready, norm + b + 1)
                nc.vector.scalar_tensor_tensor(out=temp, in0=psum[:, banks:banks + 4, :].rearrange("p b c -> p (b c)"),
                                               scalar=stat[:, norm + b:norm + b + 1], in1=gain,
                                               op0=ALU.mult, op1=ALU.mult).then_inc(resid, 1)
                ve.wait_ge(resid, count)
                nc.vector.tensor_tensor(xbuf[:, b, :], xbuf[:, b, :], temp, ALU.add).then_inc(resid, 1)

            ve.wait_ge(x_again_landed, 16 * TB)
            ve.wait_ge(gains2_landed, 32)
            temps = (wide(WP0), wide(MIX))
            for b in range(TB):
                residual(b, 4 * b, 2, wide(Q0), temps[b], 2 * b + 1)
            for b in range(TB):
                ve.wait_ge(rms_ready, 4 + b + 1)
                nc.vector.scalar_tensor_tensor(out=temps[b], in0=xbuf[:, b, :], scalar=stat[:, 4 + b:5 + b], in1=wide(D0),
                                               op0=ALU.mult, op1=ALU.mult).then_inc(normed, 1)
            act_low(8)

            gate, conv, up = pads[:, 0, PAD - 1:PAD + S + 1], pads[:, 1, 0:S], pads[:, 2, 0:S]

            def ffn_tile(i, ct):
                t = i * 2 + ct
                c = 2 * ct
                ve.wait_ge(half_ready, i * RING + (U_OUT + c + 1))
                nc.vector.tensor_tensor(gate[:, 1:1 + S], psum[:, c, 0:S], half[:, 0, :], ALU.add).then_inc(result_ready, 1)
                ve.wait_ge(result_ready, i * RING + (U_OUT + c + 1))
                nc.vector.tensor_scalar(conv, gate[:, 0:S], cols[:, bass.ds(i * 2 + (CW0 + ct), 1)], None, ALU.mult).then_inc(conv_step, 1)
                ve.wait_ge(conv_step, i * 4 + (2 * ct + 1))
                nc.vector.scalar_tensor_tensor(out=conv, in0=gate[:, 1:1 + S], scalar=cols[:, bass.ds(i * 2 + (CW1 + ct), 1)], in1=conv,
                                               op0=ALU.mult, op1=ALU.add).then_inc(conv_step, 1)
                ve.wait_ge(conv_step, i * 4 + (2 * ct + 2))
                nc.vector.scalar_tensor_tensor(out=conv, in0=gate[:, 2:2 + S], scalar=cols[:, bass.ds(i * 2 + (CW2 + ct), 1)], in1=conv,
                                               op0=ALU.mult, op1=ALU.add).then_inc(conv_ready, 1)
                split(i * RING + (U_FFN + RING + c), c)
                ve.wait_ge(half_ready, i * RING + (U_OUT + c + 2))
                nc.vector.tensor_tensor(up, psum[:, c + 1, 0:S], half[:, 1, :], ALU.add).then_inc(result_ready, 1)
                ve.wait_ge(result_ready, i * RING + (U_OUT + c + 2))
                ve.wait_ge(gelu_ready, i * 2 + (ct + 1))
                nc.vector.tensor_tensor(late[:, i * 2 + ct, :], up, conv, ALU.mult).then_inc(hidden_ready, 1)
                split(i * RING + (U_FFN + RING + c + 1), c + 1)

            with ve.Fori(0, FT // 2 - 1) as i:
                for ct in range(2):
                    ffn_tile(i, ct)
            for ct in range(2):
                ffn_tile(FT // 2 - 1, ct)
                for c in (2 * ct, 2 * ct + 1):
                    split_pair(c, c, KT + c + 1)

            with ve.Fori(0, FT // RING - 1) as i:
                for c in range(RING):
                    split(i * RING + (U_DOWN + RING + c), c)
                    split_pair(i * RING + (RING + c), c, i * RING + (KT + RING + c + 1))

            ve.wait_ge(gain3_landed, 16)
            for b in range(TB):
                residual(b, 4 - 4 * b, 6, wide(0), wide(16 + 8 * b), 2 * TB + 2 * b + 1)

        @block.gpsimd
        def _(gp):
            def rms(k):
                gp.wait_ge(squares, k + 1)
                nc.gpsimd.tensor_scalar(stat[:, k:k + 1], stat[:, k:k + 1], 1.0 / D, EPS, ALU.mult, ALU.add).then_inc(rms_step, 1)
                gp.wait_ge(rms_step, k + 1)
                nc.gpsimd.tensor_tensor(stat[:, k:k + 1], stat[:, k:k + 1], expo[:, :], ALU.pow).then_inc(rms_ready, 1)

            gp.wait_ge(exp_set, 1)
            for b in range(TB):
                rms(b)
            gp.wait_ge(pads_zero, 1)
            gp.wait_ge(pool_const_landed, 32)
            step = 0

            for m in range(8):
                c = 7 - m
                g = c // 2
                gp.wait_ge(result_ready, U_POOL + m + 1)
                source = pads[:, m % 2, :]
                now = source
                w = 1
                while w < WINDOWS[g]:
                    back, ahead = (1, 0) if w == 1 else (w // 2, w // 2)
                    a, b = PAD - REACH[w], PAD + S + REACH[w]
                    to = pads[:, 2 + (w.bit_length() % 2), :]
                    nc.gpsimd.tensor_tensor(to[:, a:b], now[:, a - back:b - back], now[:, a + ahead:b + ahead],
                                            ALU.add).then_inc(pool_step, 1)
                    step += 1
                    gp.wait_ge(pool_step, step)
                    now, w = to, 2 * w
                other = pads[:, 2 + (w.bit_length() % 2), 0:S]
                nc.gpsimd.tensor_tensor(other, now[:, PAD:PAD + S], inv_count[:, g, :], ALU.mult).then_inc(pool_step, 1)
                step += 1
                gp.wait_ge(pool_step, step)
                nc.gpsimd.tensor_tensor(late[:, D0 + c, :], other, source[:, PAD:PAD + S], ALU.subtract).then_inc(diff_ready, 1)
                gp.wait_ge(diff_ready, m + 1)
            for k in range(2, 8):
                rms(k)


NAMES = ["x", "norm_pre_mix", "w_in", "w_pool", "pool_scale", "attn_sink", "w_out", "norm_post_mix", "norm_pre_ffn",
         "w_gate", "w_up", "conv_w", "conv_b", "w_down", "norm_post_ffn"]


def shape_constants():
    q, k = np.arange(S)[:, None], np.arange(S)[None, :]
    d = np.abs(q - k).astype(np.float32)
    d = np.where(d <= WINDOW, d, np.float32(FAR)).astype(np.float32).reshape(TB, P, S)
    t = np.arange(S)
    count = [np.clip(t + w // 2, 0, S) - np.clip(t - w // 2, 0, S) for w in WINDOWS]
    inv = (np.float32(1) / np.stack(count).astype(np.float32)).astype(np.float32)
    return {"identity": np.eye(P, dtype=np.float32), "distance": d, "inverse_count": inv}


def kernel(**inputs):
    import concourse.bacc as bacc
    from concourse.bass_utils import run_bass_kernel_spmd

    nc = bacc.Bacc("TRN2", target_bir_lowering=False, num_devices=1)
    arrays, args = {}, []
    for name, a in [(n, inputs[n]) for n in NAMES] + list(shape_constants().items()):
        a = np.ascontiguousarray(a)
        arrays[f"in_{name}"] = a
        args.append(nc.dram_tensor(f"in_{name}", a.shape, mybir.dt.from_np(a.dtype), kind="ExternalInput").ap())
    args.append(nc.dram_tensor("out_y", (1, S, D), F32, kind="ExternalOutput").ap())
    layer(nc, *args)
    r = run_bass_kernel_spmd(nc, [arrays], core_ids=[0])
    return r.results[0]["out_y"]
```

```python
from contextlib import ExitStack

import numpy as np
import concourse.bass as bass
from concourse import mybir

F32 = mybir.dt.float32
F32R = mybir.dt.float32r
ALU = mybir.AluOpType
ACT = mybir.ActivationFunctionType
AX_X = mybir.AxisListType.X

P = 128
D = 2048
S = 256
TB = S // P
KT = D // P
POOL_W = D // 2
WINDOWS = (2, 4, 8, 16)
HD = 64
NQ = (D - POOL_W) // HD
NKV = NQ // 4
KV_W = NKV * HD
IN_W = POOL_W + NQ * HD + 2 * KV_W
WINDOW = 128
FF = D * 11 // 4
FT = FF // P
EPS = 1e-6
FAR = 1e33

RING = 4
U_Q, U_POOL, U_OUT = 4, 12, 20
U_FFN = U_OUT + KT
U_DOWN = U_FFN + 2 * FT
UNITS = U_DOWN + FT
PAD = max(WINDOWS) // 2
PW = S + 2 * PAD
LC = 4
NC, CW = 2, D // 2
SQUARES = [(0, 0, 2), (0, 1, 2), (1, 0, 4), (2, 0, 2), (1, 1, 4), (2, 1, 2), (3, 0, 4), (3, 1, 4)]
REACH = {1: 7, 2: 6, 4: 4, 8: 0}
SLOPES = [float(np.float32(2.0) ** np.float32(-8.0 * (h + 1) / NQ)) for h in range(NQ)]

MIX = 0
Q0, D0, WP0, K0 = 16, 24, 32, 40


def layer(nc, x, norm_pre_mix, w_in, w_pool, pool_scale, attn_sink, w_out, norm_post_mix,
          norm_pre_ffn, w_gate, w_up, conv_w, conv_b, w_down, norm_post_ffn,
          identity, distance, inverse_count, out):
    x_rows = x.rearrange("a (b p) d -> (a b) p d", p=P)
    out_rows = out.rearrange("a (b p) d -> (a b) p d", p=P)
    w_in_v = w_in.rearrange("l (k p) n -> p (l k) n", p=P)
    w_gate_v = w_gate.rearrange("l (k p) n -> p (l k) n", p=P)
    w_up_v = w_up.rearrange("l (k p) n -> p (l k) n", p=P)
    w_out_v = w_out.rearrange("l (k p) n -> p (l k) n", p=P)
    w_down_v = w_down.rearrange("l (k p) n -> p (l k) n", p=P)
    w_pool_v = w_pool.rearrange("l g (c p) d -> p (l g c) d", p=P)

    with ExitStack() as ctx:
        def sb(name, shape, dt=F32):
            return ctx.enter_context(nc.sbuf_tensor(name, shape, dt))

        def sem(name):
            return ctx.enter_context(nc.semaphore(name))

        raw = sb("raw", [P, RING, D])
        hi = sb("hi", [P, RING, D], F32R)
        lo = sb("lo", [P, RING, D], F32R)
        act = sb("act", [P, KT, 2 * S], F32R)
        pair = sb("pair", [P, RING, 2 * S], F32R)
        xbuf = sb("xbuf", [P, TB, D])
        late = sb("late", [P, FT, S])
        pads = sb("pads", [P, 4, PW])
        half = sb("half", [P, 2, S])
        dist = sb("dist", [P, TB, S])
        ident = sb("ident", [P, P])
        rows_a = sb("rows_a", [P, P])
        rows_b = sb("rows_b", [P, P])
        cols = sb("cols", [P, 4 * FT + 8])
        sink = sb("sink", [P, NQ])
        neg_sink = sb("neg_sink", [P, NQ])
        part = sb("part", [P, 8, 4])
        rstd = sb("rstd", [P, 8])
        ones = sb("ones", [1, P])
        expo = sb("expo", [P, 1])
        small = sb("small", [P, 2, 6, 4])
        psum = ctx.enter_context(nc.psum_tensor("psum", [P, 8, 512], F32))

        xflat = xbuf[:, :, :].rearrange("p b d -> p (b d)")
        prob = [xflat[:, 1024 * b:1024 * (b + 1)].rearrange("p (h s) -> p h s", h=4) for b in range(2)]
        prob_t = xflat[:, 2048:3072].rearrange("p (k c) -> p k c", k=2)
        val = xflat[:, 3072:3584].rearrange("p (b c) -> p b c", b=2)
        val_t = xflat[:, 3584:4096].rearrange("p (u s) -> p u s", u=2)
        wide = lambda a, n=8: late[:, a:a + n, :].rearrange("p t s -> p (t s)")
        inv_count = late[:, MIX:MIX + 4, :]
        gain_row = late[0:1, Q0:Q0 + 8, :].rearrange("p t s -> p (t s)")
        conv_row = pads[:, 1, 0:S]
        CW0, CW1, PS, CW2, CB = 0, FT, 2 * FT, 2 * FT + 8, 3 * FT + 8

        raw_landed = [sem(f"raw_landed_{s}") for s in range(RING)]
        x_landed = [sem(f"x_landed_{k}") for k in range(TB * NC)]
        gain_landed = sem("gain_landed")
        gain_spread = sem("gain_spread")
        ident_landed = sem("ident_landed")
        dist_landed = sem("dist_landed")
        rows_landed = sem("rows_landed")
        sink_landed = sem("sink_landed")
        count_landed = sem("count_landed")
        w_pool_landed = sem("w_pool_landed")
        x_again_landed = sem("x_again_landed")
        gains2_landed = sem("gains2_landed")
        gain3_landed = sem("gain3_landed")
        stored = sem("stored")
        hi_ready = sem("hi_ready")
        lo_ready = sem("lo_ready")
        unit_done = sem("unit_done")
        pair_hi = sem("pair_hi")
        pair_lo = sem("pair_lo")
        half_ready = sem("half_ready")
        result_ready = sem("result_ready")
        y_done = sem("y_done")
        squares = sem("squares")
        rms_ready = sem("rms_ready")
        rms_step = sem("rms_step")
        consts_set = sem("consts_set")
        normed = sem("normed")
        turned = sem("turned")
        act_hi = sem("act_hi")
        act_lo = sem("act_lo")
        val_turned = sem("val_turned")
        val_ready = sem("val_ready")
        sink_ready = sem("sink_ready")
        pads_zero = sem("pads_zero")
        scores_done = sem("scores_done")
        logits_ready = sem("logits_ready")
        max_step = sem("max_step")
        bias_ready = sem("bias_ready")
        exps_ready = sem("exps_ready")
        sum_step = sem("sum_step")
        prob_ready = sem("prob_ready")
        prob_turned = sem("prob_turned")
        prob_t_ready = sem("prob_t_ready")
        heads_done = sem("heads_done")
        heads_ready = sem("heads_ready")
        scaled = sem("scaled")
        pool_step = sem("pool_step")
        diff_ready = sem("diff_ready")
        pooled = sem("pooled")
        pooled_ready = sem("pooled_ready")
        resid = sem("resid")
        conv_step = sem("conv_step")
        conv_ready = sem("conv_ready")
        gelu_ready = sem("gelu_ready")
        hidden_ready = sem("hidden_ready")

        block = ctx.enter_context(nc.Block())

        @block.sync
        def _(sp):
            def load(n, c, src):
                if not isinstance(n, int) or n >= RING:
                    sp.wait_ge(lo_ready, n - RING + 1)
                dst = raw[:, c, :]
                if len(src.shape) == 3:
                    dst = dst.rearrange("p (k n) -> p k n", k=KT)
                sp.dma_start(dst, src).then_inc(raw_landed[c], 16)

            def in_columns(first):
                return w_in_v[:, :, first:first + P]

            def spread(a, gain, landed):
                sp.dma_start(wide(a), gain.partition_broadcast(P).rearrange("p l d -> p (l d)")).then_inc(landed, 16)

            firsts = (IN_W - 2 * KV_W, IN_W - 2 * KV_W + P, IN_W - KV_W, IN_W - KV_W + P)
            for b in range(TB):
                for h in range(NC):
                    sp.dma_start(xbuf[:, b, h * CW:(h + 1) * CW], x_rows[b][:, h * CW:(h + 1) * CW]).then_inc(x_landed[NC * b + h], 16)
                load(b, b, in_columns(firsts[b]))
            for c in (2, 3):
                load(c, c, in_columns(firsts[c]))
            with sp.Fori(0, 2) as i:
                for c in range(RING):
                    load(i * RING + (U_Q + c), c, w_in_v[:, :, bass.ds(i * (RING * P) + (POOL_W + c * P), P)])
            sp.dma_start(late[:, WP0:WP0 + 8, :], w_pool_v).then_inc(w_pool_landed, 16)
            for m in range(8):
                load(U_POOL + m, m % RING, in_columns((7 - m) * P))
            for r in range(KT):
                if r == 6:
                    sp.wait_ge(heads_done, 8)
                    for b in range(TB):
                        sp.dma_start(xbuf[:, b, :], x_rows[b]).then_inc(x_again_landed, 16)
                    sp.wait_ge(pooled, 4)
                    spread(Q0, norm_post_mix, gains2_landed)
                    spread(D0, norm_pre_ffn, gains2_landed)
                load(U_OUT + r, r % RING, w_out_v[:, (r + 8) % KT, :])
            with sp.Fori(0, FT // 2) as i:
                for c in range(RING):
                    w = (w_gate_v, w_up_v)[c % 2]
                    load(i * RING + (U_FFN + c), c, w[:, :, bass.ds(i * (2 * P) + (c // 2) * P, P)])
            with sp.Fori(0, FT // RING - 1) as i:
                for c in range(RING):
                    load(i * RING + (U_DOWN + c), c, w_down_v[:, i * RING + c, :])
            sp.wait_ge(pair_lo, KT + 24)
            spread(16, norm_post_ffn, gain3_landed)
            for c in range(RING):
                load(UNITS - RING + c, c, w_down_v[:, FT - RING + c, :])
            for k in range(2 * LC):
                b, h = k // LC, k % LC
                sp.wait_ge(resid, 2 * NC + k + 1)
                sp.dma_start(out_rows[b][:, h * 512:(h + 1) * 512], xbuf[:, b, h * 512:(h + 1) * 512]).then_inc(stored, 16)
            sp.wait_ge(stored, 16 * 2 * LC)

        @block.tensor
        def _(pe):
            def turn(norm, b, source):
                for kt in range(KT):
                    if kt % 8 == 0:
                        pe.wait_ge(normed, NC * (TB * norm + b) + kt // 8 + 1)
                    mm = nc.tensor.transpose(psum[:, 4 * b + kt // 4, (kt % 4) * P:(kt % 4 + 1) * P],
                                             source[:, kt * P:(kt + 1) * P], ident[:, :])
                    if kt % 4 == 3:
                        mm.then_inc(turned, 1)

            def block_column_unit(n, c, b, norm):
                if b == 0:
                    pe.wait_ge(lo_ready, n + 1)
                t, both = slice(b * P, (b + 1) * P), "p (h b s) -> p h b s"
                out_both = psum[:, c, :].rearrange(both, h=2, b=TB)[:, :, b, :]
                for kt in range(KT):
                    if c == 0 and kt % 4 == 0:
                        pe.wait_ge(act_lo, 8 * norm + 4 * b + kt // 4 + 1)
                    high = (hi[:, c, kt * P:(kt + 1) * P], act[:, kt, :].rearrange(both, h=2, b=TB)[:, :, b, :], out_both)
                    low = (lo[:, c, kt * P:(kt + 1) * P], act[:, kt, t], psum[:, c, t])
                    last = kt == KT - 1
                    for k, (w, a, o) in enumerate((low, high) if last else (high, low)):
                        mm = nc.tensor.matmul(o, w, a, start=(kt == 0 and k == 0), stop=(last and k == 1))
                if b == TB - 1:
                    mm.then_inc(unit_done, 1)

            def first_column_units(n, norm, sources, second):
                turn(norm, 0, sources[0])
                for c in range(RING):
                    if c == second:
                        turn(norm, 1, sources[1])
                    block_column_unit(n + c, c, 0, norm)
                for c in range(RING):
                    block_column_unit(n + c, c, 1, norm)

            def column_unit(n, c, bank, free_after):
                pe.wait_ge(lo_ready, n + 1)
                pe.wait_ge(result_ready, free_after)
                for kt in range(KT):
                    high = (hi[:, c, kt * P:(kt + 1) * P], act[:, kt, :], psum[:, bank, :])
                    low = (lo[:, c, kt * P:(kt + 1) * P], act[:, kt, 0:S], psum[:, bank, 0:S])
                    last = kt == KT - 1
                    for k, (w, a, o) in enumerate((low, high) if last else (high, low)):
                        mm = nc.tensor.matmul(o, w, a, start=(kt == 0 and k == 0), stop=(last and k == 1))
                mm.then_inc(unit_done, 1)

            def rows_of_block(c, b, bank, start, stop):
                for j in range(4):
                    o = psum[:, bank + j, :]
                    a_hi, a_lo = (pair[:, c, k * S + b * P:k * S + (b + 1) * P] for k in range(2))
                    w_hi, w_lo = (w[:, c, j * 512:(j + 1) * 512] for w in (hi, lo))
                    nc.tensor.matmul(o, a_hi, w_hi, start=start, stop=False)
                    nc.tensor.matmul(o, a_hi, w_lo, start=False, stop=False)
                    mm = nc.tensor.matmul(o, a_lo, w_hi, start=False, stop=stop)
                    if stop and (b, j) != (TB - 1, 3):
                        mm.then_inc(y_done, 1)
                return mm

            def row_unit(n, c, pairs, start, banks, second_free=None):
                pe.wait_ge(lo_ready, n + 1)
                pe.wait_ge(pair_lo, pairs)
                rows_of_block(c, 0, banks[0], start, False)
                if second_free is not None:
                    pe.wait_ge(result_ready, second_free)
                rows_of_block(c, 1, banks[1], start, False).then_inc(unit_done, 1)

            def last_row_units(n, pairs, banks):
                for b in range(TB):
                    for c in range(RING):
                        if b == 0:
                            pe.wait_ge(lo_ready, n + c + 1)
                            pe.wait_ge(pair_lo, pairs + c + 1)
                        mm = rows_of_block(c, b, banks[b], False, c == RING - 1)
                        if b == TB - 1:
                            mm.then_inc(unit_done, 1)

            def scores(m):
                if m >= 1:
                    pe.wait_ge(logits_ready, m)
                j, qb = m // 2, m % 2
                for e in range(2):
                    for t in range(2):
                        r = slice(64 * e, 64 * e + 64)
                        mm = nc.tensor.matmul(psum[:, 4 + e, t * S:(t + 1) * S],
                                              late[r, Q0 + 2 * j + t, qb * P:(qb + 1) * P],
                                              late[r, K0 + j, :], start=True, stop=True)
                mm.then_inc(scores_done, 1)

            def turn_probs(m):
                pe.wait_ge(prob_ready, m + 1)
                if m >= 1:
                    pe.wait_ge(prob_t_ready, m)
                for kb in range(2):
                    for hh in range(4):
                        mm = nc.tensor.transpose(psum[:, 6 + kb, hh * P:(hh + 1) * P],
                                                 prob[m % 2][:, hh, kb * P:(kb + 1) * P], ident[:, :])
                mm.then_inc(prob_turned, 1)

            def heads(m):
                pe.wait_ge(prob_t_ready, m + 1)
                if m >= 2:
                    pe.wait_ge(heads_ready, m - 1)
                j = m // 2
                for e in range(2):
                    for kb in range(2):
                        rhs = prob_t[:, kb, :].rearrange("p (t e q) -> p t e q", t=2, e=2)[:, :, e, :]
                        mm = nc.tensor.matmul(psum[64 * e:64 * e + 64, 2 + m % 2, 0:S],
                                              val[:, kb, j * HD:(j + 1) * HD], rhs,
                                              start=(kb == 0), stop=(kb == 1))
                mm.then_inc(heads_done, 1)

            pe.wait_ge(gain_landed, 16)
            pe.wait_ge(consts_set, 1)
            for j in range(4):
                mm = nc.tensor.matmul(psum[:, 4 + j, :], ones[:, :], gain_row[:, j * 512:(j + 1) * 512], start=True, stop=True)
            mm.then_inc(gain_spread, 1)
            pe.wait_ge(ident_landed, 16)
            first_column_units(0, 0, [xbuf[:, b, :] for b in range(TB)], 1)
            with pe.Fori(0, 2) as i:
                for c in range(RING):
                    column_unit(i * RING + (U_Q + c), c, c, i * RING + (U_Q + c - RING + 1))
            pe.wait_ge(result_ready, U_Q)
            for tb in range(TB):
                for u in range(2):
                    nc.tensor.transpose(psum[:, 6, (tb * 2 + u) * P:(tb * 2 + u + 1) * P],
                                        val_t[:, u, tb * P:(tb + 1) * P], ident[:, :])
            pe.wait_ge(rows_landed, 16 * 5)
            nc.tensor.transpose(psum[:, 7, 0:2 * FT + 8], rows_a[0:2 * FT + 8, :], ident[0:2 * FT + 8, 0:2 * FT + 8])
            nc.tensor.transpose(psum[:, 7, 2 * FT + 8:4 * FT + 8], rows_b[0:2 * FT, :],
                                ident[0:2 * FT, 0:2 * FT]).then_inc(val_turned, 1)
            for m in range(8):
                if m == 0:
                    pe.wait_ge(result_ready, U_POOL)
                scores(m)
                n = U_POOL + m
                column_unit(n, n % RING, n % 2, U_POOL if m < 2 else n - 1)
                if m >= 2:
                    heads(m - 2)
                if m == 1:
                    pe.wait_ge(val_ready, 2)
                if m >= 1:
                    turn_probs(m - 1)
            heads(6)
            turn_probs(7)
            pe.wait_ge(w_pool_landed, 16)
            for k, g in enumerate((3, 2, 1, 0)):
                pe.wait_ge(diff_ready, 2 * k + 2)
                if k == 0:
                    pe.wait_ge(result_ready, U_OUT)
                    pe.wait_ge(logits_ready, 8)
                for mt in range(2):
                    for kc in range(2):
                        mm = nc.tensor.matmul(psum[:, (0, 1, 4, 5)[g], mt * S:(mt + 1) * S],
                                              late[:, WP0 + 2 * g + kc, mt * P:(mt + 1) * P],
                                              late[:, D0 + 2 * g + kc, :], start=(kc == 0), stop=(kc == 1))
                mm.then_inc(pooled, 1)
            heads(7)

            pe.wait_ge(pooled_ready, 8)
            pe.wait_ge(heads_ready, 8)
            for r in range(KT - RING):
                row_unit(U_OUT + r, r % RING, r + 1, r == 0, (0, 4))
            last_row_units(U_FFN - RING, KT - RING, (0, 4))
            pe.wait_ge(scaled, NC)

            first_column_units(U_FFN, 1, [wide(WP0), wide(MIX)], 3)
            with pe.Fori(1, FT // 2) as i:
                for c in range(RING):
                    column_unit(i * RING + (U_FFN + c), c, c, i * RING + (U_OUT + c - RING + 1))

            for c in range(RING):
                row_unit(U_DOWN + c, c, KT + c + 1, c == 0, (4, 0), U_OUT + 2 * FT if c == 0 else None)
            with pe.Fori(1, FT // RING - 1) as i:
                for c in range(RING):
                    row_unit(i * RING + (U_DOWN + c), c, i * RING + (KT + c + 1), False, (4, 0))
            last_row_units(UNITS - RING, KT + FT - RING, (4, 0))

        @block.scalar
        def _(sc):
            def split(n, c):
                if n >= RING:
                    sc.wait_ge(unit_done, n - RING + 1)
                sc.wait_ge(raw_landed[c], (n // RING + 1) * 16)
                nc.scalar.copy(hi[:, c, :], raw[:, c, :]).then_inc(hi_ready, 1)

            def split_looped(i, first, c):
                sc.wait_ge(unit_done, i * RING + (first + c - RING + 1))
                sc.wait_ge(raw_landed[c], i * 16 + (first // RING + 1) * 16)
                nc.scalar.copy(hi[:, c, :], raw[:, c, :]).then_inc(hi_ready, 1)

            def split_pair(tile, c):
                nc.scalar.copy(pair[:, c, 0:S], late[:, tile, :]).then_inc(pair_hi, 1)

            def half_out(n, c, bank, scale=1.0):
                sc.wait_ge(unit_done, n + 1)
                nc.scalar.activation(half[:, c % 2, :], psum[:, bank, S:2 * S], ACT.Copy, scale=scale).then_inc(half_ready, 1)

            def act_high(norm, b):
                for k in range(4):
                    sc.wait_ge(turned, 8 * norm + 4 * b + k + 1)
                    nc.scalar.copy(act[:, 4 * k:4 * k + 4, b * P:(b + 1) * P],
                                   psum[:, 4 * b + k, :].rearrange("p (t s) -> p t s", t=4)).then_inc(act_hi, 1)

            def squares_of(norm, b, wait, source):
                first, n = squares_before(norm, b)
                for k in range(n):
                    wait(k)
                    if first + k >= 2:
                        sc.wait_ge(squares, first + k - 1)
                    w = D // n
                    nc.scalar.activation(scratch[(first + k) % 2][:, 0:w], source(k, w), ACT.Square,
                                         accum_out=part[:, TB * norm + b, k:k + 1]).then_inc(squares, 1)

            scratch = [wide(MIX + 8 + 4 * k, 4) for k in range(2)]

            def squares_of_x(norm, b):
                squares_of(norm, b, lambda k: sc.wait_ge(*((x_landed[NC * b + k], 16) if norm == 0 else (resid, NC * b + k + 1))),
                           lambda k, w: xbuf[:, b, k * w:(k + 1) * w])

            def squares_of_y(norm, b, bank, product, last_unit):
                squares_of(norm, b, lambda k: sc.wait_ge(*((unit_done, last_unit + 1) if (b, k) == (TB - 1, 3)
                                                           else (y_done, 7 * product + 4 * b + k + 1))),
                           lambda k, w: psum[:, bank + k, :])

            sc.dma_start(gain_row, norm_pre_mix).then_inc(gain_landed, 16)
            sc.dma_start(ident[:, :], identity).then_inc(ident_landed, 16)
            for b in range(TB):
                squares_of_x(0, b)
                split(b, b)
            act_high(0, 0)
            for k, (dst, a, src) in enumerate(((rows_a, 0, conv_w[0, 0]), (rows_a, FT, conv_w[0, 1]), (rows_a, 2 * FT, pool_scale[0]),
                                               (rows_b, 0, conv_w[0, 2]), (rows_b, FT, conv_b[0]))):
                t = src.shape[0] // P
                sc.dma_start(dst[a:a + t, :], src.rearrange("(t p) -> t p", p=P)).then_inc(rows_landed, 16)
            sc.dma_start(sink[:, :], attn_sink.partition_broadcast(P).rearrange("p l h -> p (l h)")).then_inc(sink_landed, 16)
            split(2, 2)
            act_high(0, 1)
            split(3, 3)
            sc.dma_start(dist[:, :, :], distance.rearrange("b p s -> p b s")).then_inc(dist_landed, 16)
            sc.wait_ge(squares, 4)
            sc.dma_start(inv_count, inverse_count.partition_broadcast(P)).then_inc(count_landed, 16)

            for n in range(U_Q):
                if n >= 2:
                    sc.wait_ge(result_ready, n - 1)
                half_out(n, n, n)
                split(n + RING, n % RING)
            with sc.Fori(0, 2) as i:
                for c in range(RING):
                    sc.wait_ge(result_ready, i * RING + (U_Q + c - 1))
                    half_out(i * RING + (U_Q + c), c, c, HD ** -0.5)
                    split_looped(i, 2 * RING, c)
            sc.wait_ge(val_turned, 1)
            nc.scalar.copy(val, psum[:, 6, :].rearrange("p (b c) -> p b c", b=2)).then_inc(val_ready, 1)
            nc.scalar.copy(cols[:, :], psum[:, 7, 0:4 * FT + 8]).then_inc(val_ready, 1)

            def exps(m):
                sc.wait_ge(bias_ready, m + 1)
                s = small[:, m % 2]
                for hh in range(4):
                    h = prob[m % 2][:, hh, :]
                    nc.scalar.activation(h, h, ACT.Exp, bias=s[:, 1, hh:hh + 1], accum_out=s[:, 3, hh:hh + 1])
                nc.scalar.activation(s[:, 4, :], s[:, 2, :], ACT.Exp).then_inc(exps_ready, 1)

            def probs_out(m):
                sc.wait_ge(prob_turned, m + 1)
                if m >= 1:
                    sc.wait_ge(heads_done, m)
                nc.scalar.copy(prob_t, psum[:, 6:8, :]).then_inc(prob_t_ready, 1)

            def heads_out(m):
                sc.wait_ge(heads_done, m + 1)
                j, qb = m // 2, m % 2
                nc.scalar.copy(late[:, MIX + 8 + 2 * j:MIX + 10 + 2 * j, qb * P:(qb + 1) * P],
                               psum[:, 2 + m % 2, 0:S].rearrange("p (t q) -> p t q", t=2)).then_inc(heads_ready, 1)

            for m in range(8):
                n = U_POOL + m
                exps(m)
                sc.wait_ge(result_ready, n - 1)
                half_out(n, n, n % 2)
                if m >= 2:
                    heads_out(m - 2)
                if m >= 1:
                    probs_out(m - 1)
                split(n + RING, n % RING)
                if m >= RING:
                    r = m - RING
                    sc.wait_ge(heads_ready, 2 * (r // 2) + 2)
                    split_pair(MIX + 8 + r, r)
            heads_out(6)
            probs_out(7)
            for k, g in enumerate((3, 2, 1, 0)):
                sc.wait_ge(pooled, k + 1)
                if k == 0:
                    sc.wait_ge(val_ready, 2)
                    sc.wait_ge(diff_ready, 8)
                for mt in range(2):
                    t = 2 * g + mt
                    nc.scalar.activation(late[:, MIX + t, :], psum[:, (0, 1, 4, 5)[g], mt * S:(mt + 1) * S], ACT.Copy,
                                         scale=cols[:, PS + t:PS + t + 1]).then_inc(pooled_ready, 1)
            heads_out(7)

            for r in range(KT - RING):
                split(U_OUT + r + RING, r % RING)
                if r == 0:
                    sc.wait_ge(heads_ready, 8)
                    sc.wait_ge(pooled_ready, 8)
                split_pair(MIX + (r + RING + 8) % KT, r % RING)

            sc.wait_ge(pair_lo, KT)
            squares_of_y(1, 0, 0, 0, U_FFN - 1)
            squares_of_x(2, 0)
            split(U_FFN, 0)
            split(U_FFN + 1, 1)
            split(U_FFN + 2, 2)
            squares_of_y(1, 1, 4, 0, U_FFN - 1)
            split(U_FFN + 3, 3)
            act_high(1, 0)
            squares_of_x(2, 1)
            act_high(1, 1)

            def ffn_tile(i, ct):
                c = 2 * ct
                sc.wait_ge(result_ready, i * RING + (U_OUT + c - 1))
                half_out(i * RING + (U_FFN + c), c, c)
                split_looped(i, U_FFN + RING, c)
                sc.wait_ge(conv_ready, i * 2 + (ct + 1))
                nc.scalar.activation(conv_row, conv_row, ACT.Gelu_apprx_tanh,
                                     bias=cols[:, bass.ds(i * 2 + (CB + ct), 1)]).then_inc(gelu_ready, 1)
                sc.wait_ge(result_ready, i * RING + (U_OUT + c))
                half_out(i * RING + (U_FFN + c + 1), c + 1, c + 1)
                split_looped(i, U_FFN + RING, c + 1)

            with sc.Fori(0, FT // 2 - 1) as i:
                for ct in range(2):
                    ffn_tile(i, ct)
            for c in range(RING):
                sc.wait_ge(hidden_ready, c + 1)
                split_pair(c, c)
            for ct in range(2):
                ffn_tile(FT // 2 - 1, ct)

            with sc.Fori(0, FT // RING - 1) as i:
                for c in range(RING):
                    split_looped(i, U_DOWN + RING, c)
                    if c == 0:
                        sc.wait_ge(hidden_ready, FT)
                    split_pair(i * RING + (RING + c), c)

            sc.wait_ge(pair_lo, KT + 16)
            squares_of_y(3, 0, 4, 1, UNITS - 1)
            squares_of_y(3, 1, 0, 1, UNITS - 1)

        @block.vector
        def _(ve):
            def split(n, c):
                ve.wait_ge(hi_ready, n + 1)
                nc.vector.tensor_tensor(lo[:, c, :], raw[:, c, :], hi[:, c, :].bitcast(F32), ALU.subtract).then_inc(lo_ready, 1)

            def split_pair(tile, c, count):
                ve.wait_ge(pair_hi, count)
                nc.vector.tensor_tensor(pair[:, c, S:2 * S], late[:, tile, :], pair[:, c, 0:S].bitcast(F32),
                                        ALU.subtract).then_inc(pair_lo, 1)

            def act_low(norm, b):
                for k in range(4):
                    at = act[:, 4 * k:4 * k + 4, :]
                    ve.wait_ge(act_hi, 8 * norm + 4 * b + k + 1)
                    nc.vector.tensor_tensor(at[:, :, S + b * P:S + (b + 1) * P],
                                            psum[:, 4 * b + k, :].rearrange("p (t s) -> p t s", t=4),
                                            at[:, :, b * P:(b + 1) * P].bitcast(F32), ALU.subtract).then_inc(act_lo, 1)

            def norm_rows(norm, slot, b, to, gain):
                ve.wait_ge(rms_ready, slot)
                for h in range(NC):
                    w = slice(h * CW, (h + 1) * CW)
                    nc.vector.scalar_tensor_tensor(out=to[:, w], in0=xbuf[:, b, w], scalar=rstd[:, TB * norm + b:TB * norm + b + 1],
                                                   in1=gain[:, w], op0=ALU.mult, op1=ALU.mult).then_inc(normed, 1)

            nc.vector.memset(expo[:, :], -0.5)
            nc.vector.memset(ones[:, :], 1.0).then_inc(consts_set, 1)
            nc.vector.memset(pads[:, :, :], 0.0).then_inc(pads_zero, 1)
            ve.wait_ge(gain_spread, 1)
            gain0 = psum[:, 4:8, :].rearrange("p b c -> p (b c)")
            norm_rows(0, 1, 0, xbuf[:, 0, :], gain0)
            split(0, 0)
            norm_rows(0, 2, 1, xbuf[:, 1, :], gain0)
            act_low(0, 0)
            split(1, 1)
            split(2, 2)
            act_low(0, 1)
            split(3, 3)
            ve.wait_ge(sink_landed, 16)
            nc.vector.tensor_scalar(neg_sink[:, :], sink[:, :], -1.0, None, ALU.mult).then_inc(sink_ready, 1)

            for n in range(2):
                ve.wait_ge(half_ready, n + 1)
                for e in range(2):
                    for to in range(2):
                        s, r = slice(64 * e, 64 * e + 64), slice(64 * to, 64 * to + 64)
                        op = nc.vector.tensor_tensor(late[r, K0 + 2 * n + e, :], psum[s, n, 0:S], half[s, n, :], ALU.add)
                op.then_inc(result_ready, 1)
                if n:
                    split(n + 3, (n + 3) % RING)
            for n in range(2, 4):
                ve.wait_ge(half_ready, n + 1)
                nc.vector.tensor_tensor(val_t[:, n - 2, :], psum[:, n, 0:S], half[:, n % 2, :], ALU.add).then_inc(result_ready, 1)
                split(n + 3, (n + 3) % RING)
            with ve.Fori(0, 2) as i:
                for c in range(RING):
                    ve.wait_ge(half_ready, i * RING + (U_Q + c + 1))
                    nc.vector.scalar_tensor_tensor(out=late[:, i * RING + (Q0 + c), :], in0=psum[:, c, 0:S], scalar=HD ** -0.5,
                                                   in1=half[:, c % 2, :], op0=ALU.mult, op1=ALU.add).then_inc(result_ready, 1)
                    split(i * RING + (U_Q + c + 3), (c + 3) % RING)

            ve.wait_ge(sink_ready, 1)
            ve.wait_ge(dist_landed, 16)
            for m in range(8):
                n, j, qb = U_POOL + m, m // 2, m % 2
                s, p = small[:, m % 2], prob[m % 2]
                ve.wait_ge(scores_done, m + 1)
                if m >= 2:
                    ve.wait_ge(prob_turned, m - 1)
                for hh in range(4):
                    op = nc.vector.scalar_tensor_tensor(out=p[:, hh, :], in0=dist[:, qb, :], scalar=-SLOPES[4 * j + hh],
                                                        in1=psum[:, 4 + hh % 2, (hh // 2) * S:(hh // 2 + 1) * S],
                                                        op0=ALU.mult, op1=ALU.add)
                op.then_inc(logits_ready, 1)
                ve.wait_ge(logits_ready, m + 1)
                nc.vector.reduce_max(s[:, 0, :], p, AX_X).then_inc(max_step, 1)
                ve.wait_ge(max_step, 2 * m + 1)
                nc.vector.scalar_tensor_tensor(out=s[:, 1, :], in0=s[:, 0, :], scalar=-1.0, in1=neg_sink[:, 4 * j:4 * j + 4],
                                               op0=ALU.mult, op1=ALU.min).then_inc(max_step, 1)
                ve.wait_ge(max_step, 2 * m + 2)
                nc.vector.tensor_tensor(s[:, 2, :], s[:, 1, :], sink[:, 4 * j:4 * j + 4], ALU.add).then_inc(bias_ready, 1)
                split(n + 3, (n + 3) % RING)
                ve.wait_ge(exps_ready, m + 1)
                nc.vector.tensor_tensor(s[:, 3, :], s[:, 3, :], s[:, 4, :], ALU.add).then_inc(sum_step, 1)
                ve.wait_ge(sum_step, 2 * m + 1)
                nc.vector.reciprocal(s[:, 5, :], s[:, 3, :]).then_inc(sum_step, 1)
                ve.wait_ge(sum_step, 2 * m + 2)
                for hh in range(4):
                    op = nc.vector.tensor_scalar(p[:, hh, :], p[:, hh, :], s[:, 5, hh:hh + 1], None, ALU.mult)
                op.then_inc(prob_ready, 1)
                ve.wait_ge(half_ready, n + 1)
                if m >= 2:
                    ve.wait_ge(diff_ready, m - 1)
                nc.vector.tensor_tensor(pads[:, m % 2, PAD:PAD + S], psum[:, n % 2, 0:S], half[:, n % 2, :],
                                        ALU.add).then_inc(result_ready, 1)
                if m >= RING:
                    split_pair(MIX + 8 + m - RING, m - RING, m - RING + 1)

            for r in range(KT - 3):
                split(U_OUT + r + 3, (r + 3) % RING)
                if r + RING < KT:
                    split_pair(MIX + (r + RING + 8) % KT, r % RING, r + RING + 1)

            def scale_rows(norm, slot, b, bank, gain, temp, chunks, before):
                ve.wait_ge(rms_ready, slot)
                w = D // chunks
                y = psum[:, bank:bank + 4, :].rearrange("p b c -> p (b c)")
                for h in range(chunks + 1):
                    if h < chunks:
                        at = slice(h * w, (h + 1) * w)
                        nc.vector.scalar_tensor_tensor(out=temp[:, at], in0=y[:, at], scalar=rstd[:, TB * norm + b:TB * norm + b + 1],
                                                       in1=gain[:, at], op0=ALU.mult, op1=ALU.mult).then_inc(scaled, 1)
                    if h:
                        at = slice((h - 1) * w, h * w)
                        ve.wait_ge(scaled, before + h)
                        nc.vector.tensor_tensor(xbuf[:, b, at], xbuf[:, b, at], temp[:, at], ALU.add).then_inc(resid, 1)

            ve.wait_ge(x_again_landed, 16 * TB)
            ve.wait_ge(gains2_landed, 32)
            temps = (wide(WP0), wide(MIX))
            scale_rows(1, 3, 0, 0, wide(Q0), temps[0], NC, 0)
            split(U_FFN, 0)
            norm_rows(2, 4, 0, temps[0], wide(D0))
            split(U_FFN + 1, 1)
            act_low(1, 0)
            scale_rows(1, 5, 1, 4, wide(Q0), temps[1], NC, NC)
            split(U_FFN + 2, 2)
            norm_rows(2, 6, 1, temps[1], wide(D0))
            split(U_FFN + 3, 3)
            act_low(1, 1)

            gate, up = pads[:, 0, PAD - 1:PAD + S + 1], pads[:, 2, 0:S]
            ve.wait_ge(diff_ready, 8)

            def ffn_tile(i, ct, ahead=True):
                c = 2 * ct
                ve.wait_ge(half_ready, i * RING + (U_OUT + c + 1))
                nc.vector.tensor_tensor(gate[:, 1:1 + S], psum[:, c, 0:S], half[:, 0, :], ALU.add).then_inc(result_ready, 1)
                ve.wait_ge(result_ready, i * RING + (U_OUT + c + 1))
                nc.vector.tensor_scalar(conv_row, gate[:, 0:S], cols[:, bass.ds(i * 2 + (CW0 + ct), 1)], None, ALU.mult).then_inc(conv_step, 1)
                ve.wait_ge(conv_step, i * 4 + (2 * ct + 1))
                nc.vector.scalar_tensor_tensor(out=conv_row, in0=gate[:, 1:1 + S], scalar=cols[:, bass.ds(i * 2 + (CW1 + ct), 1)],
                                               in1=conv_row, op0=ALU.mult, op1=ALU.add).then_inc(conv_step, 1)
                ve.wait_ge(conv_step, i * 4 + (2 * ct + 2))
                nc.vector.scalar_tensor_tensor(out=conv_row, in0=gate[:, 2:2 + S], scalar=cols[:, bass.ds(i * 2 + (CW2 + ct), 1)],
                                               in1=conv_row, op0=ALU.mult, op1=ALU.add).then_inc(conv_ready, 1)
                if ahead:
                    split(i * RING + (U_FFN + c + 3), (c + 3) % RING)
                ve.wait_ge(half_ready, i * RING + (U_OUT + c + 2))
                nc.vector.tensor_tensor(up, psum[:, c + 1, 0:S], half[:, 1, :], ALU.add).then_inc(result_ready, 1)
                ve.wait_ge(result_ready, i * RING + (U_OUT + c + 2))
                ve.wait_ge(gelu_ready, i * 2 + (ct + 1))
                nc.vector.tensor_tensor(late[:, i * 2 + ct, :], up, conv_row, ALU.mult).then_inc(hidden_ready, 1)
                split(i * RING + (U_FFN + c + 4), c)

            for ct in range(2):
                ffn_tile(0, ct, ct > 0)
            with ve.Fori(1, FT // 2 - 1) as i:
                for ct in range(2):
                    ffn_tile(i, ct)
            for c in range(RING):
                split_pair(c, c, KT + c + 1)
            for ct in range(2):
                ffn_tile(FT // 2 - 1, ct)

            with ve.Fori(0, FT // RING - 1) as i:
                for c in range(RING):
                    split(i * RING + (U_DOWN + 3 + c), (c + 3) % RING)
                    split_pair(i * RING + (RING + c), c, i * RING + (KT + RING + c + 1))
            split(UNITS - 1, RING - 1)

            ve.wait_ge(gain3_landed, 16)
            for b in range(TB):
                scale_rows(3, 7 + b, b, 4 - 4 * b, wide(16), wide(24 + 8 * b), LC, NC * TB + LC * b)

        @block.gpsimd
        def _(gp):
            tiny = [0]

            def rms(slot):
                norm, b, n = SQUARES[slot]
                gp.wait_ge(squares, sum(x[2] for x in SQUARES[:slot + 1]))
                k = TB * norm + b
                total, out = part[:, k, 0:1], rstd[:, k:k + 1]

                def stepped(op):
                    op.then_inc(rms_step, 1)
                    tiny[0] += 1
                    gp.wait_ge(rms_step, tiny[0])

                if n == 4:
                    stepped(nc.gpsimd.tensor_tensor(part[:, k, 0:2], part[:, k, 0:2], part[:, k, 2:4], ALU.add))
                stepped(nc.gpsimd.tensor_tensor(total, total, part[:, k, 1:2], ALU.add))
                stepped(nc.gpsimd.tensor_scalar(total, total, 1.0 / D, EPS, ALU.mult, ALU.add))
                nc.gpsimd.tensor_tensor(out, total, expo[:, :], ALU.pow).then_inc(rms_ready, 1)

            gp.wait_ge(consts_set, 1)
            for slot in range(2):
                rms(slot)
            gp.wait_ge(pads_zero, 1)
            gp.wait_ge(count_landed, 16)
            step = 0

            for m in range(8):
                c = 7 - m
                g = c // 2
                gp.wait_ge(result_ready, U_POOL + m + 1)
                source = pads[:, m % 2, :]
                now = source
                w = 1
                while w < WINDOWS[g]:
                    back, ahead = (1, 0) if w == 1 else (w // 2, w // 2)
                    a, b = PAD - REACH[w], PAD + S + REACH[w]
                    to = pads[:, 2 + (w.bit_length() % 2), :]
                    nc.gpsimd.tensor_tensor(to[:, a:b], now[:, a - back:b - back], now[:, a + ahead:b + ahead],
                                            ALU.add).then_inc(pool_step, 1)
                    step += 1
                    gp.wait_ge(pool_step, step)
                    now, w = to, 2 * w
                other = pads[:, 2 + (w.bit_length() % 2), 0:S]
                nc.gpsimd.tensor_tensor(other, now[:, PAD:PAD + S], inv_count[:, g, :], ALU.mult).then_inc(pool_step, 1)
                step += 1
                gp.wait_ge(pool_step, step)
                nc.gpsimd.tensor_tensor(late[:, D0 + c, :], other, source[:, PAD:PAD + S], ALU.subtract).then_inc(diff_ready, 1)
                gp.wait_ge(diff_ready, m + 1)
            for slot in range(2, len(SQUARES)):
                rms(slot)


def squares_before(norm, b):
    k = [x[:2] for x in SQUARES].index((norm, b))
    return sum(x[2] for x in SQUARES[:k]), SQUARES[k][2]


NAMES = ["x", "norm_pre_mix", "w_in", "w_pool", "pool_scale", "attn_sink", "w_out", "norm_post_mix", "norm_pre_ffn",
         "w_gate", "w_up", "conv_w", "conv_b", "w_down", "norm_post_ffn"]


def shape_constants():
    q, k = np.arange(S)[:, None], np.arange(S)[None, :]
    d = np.abs(q - k).astype(np.float32)
    d = np.where(d <= WINDOW, d, np.float32(FAR)).astype(np.float32).reshape(TB, P, S)
    t = np.arange(S)
    count = [np.clip(t + w // 2, 0, S) - np.clip(t - w // 2, 0, S) for w in WINDOWS]
    inv = (np.float32(1) / np.stack(count).astype(np.float32)).astype(np.float32)
    return {"identity": np.eye(P, dtype=np.float32), "distance": d, "inverse_count": inv}


def kernel(**inputs):
    import concourse.bacc as bacc
    from concourse.bass_utils import run_bass_kernel_spmd

    nc = bacc.Bacc("TRN2", target_bir_lowering=False, num_devices=1)
    arrays, args = {}, []
    for name, a in [(n, inputs[n]) for n in NAMES] + list(shape_constants().items()):
        a = np.ascontiguousarray(a)
        arrays[f"in_{name}"] = a
        args.append(nc.dram_tensor(f"in_{name}", a.shape, mybir.dt.from_np(a.dtype), kind="ExternalInput").ap())
    args.append(nc.dram_tensor("out_y", (1, S, D), F32, kind="ExternalOutput").ap())
    layer(nc, *args)
    r = run_bass_kernel_spmd(nc, [arrays], core_ids=[0])
    return r.results[0]["out_y"]
```

```python
from contextlib import ExitStack

import numpy as np
import concourse.bass as bass
from concourse import mybir

F32 = mybir.dt.float32
F32R = mybir.dt.float32r
ALU = mybir.AluOpType
ACT = mybir.ActivationFunctionType
AX_X = mybir.AxisListType.X

P = 128
D = 2048
S = 256
TB = S // P
KT = D // P
POOL_W = D // 2
WINDOWS = (2, 4, 8, 16)
HD = 64
NQ = (D - POOL_W) // HD
NKV = NQ // 4
KV_W = NKV * HD
IN_W = POOL_W + NQ * HD + 2 * KV_W
WINDOW = 128
FF = D * 11 // 4
FT = FF // P
EPS = 1e-6
FAR = 1e33

RING = 4
U_Q, U_POOL, U_OUT = 4, 12, 20
U_FFN = U_OUT + KT
U_DOWN = U_FFN + 2 * FT
UNITS = U_DOWN + FT
PAD = max(WINDOWS) // 2
PW = S + 2 * PAD
LC = 4
NC, CW = 2, D // 2
SQUARES = [(0, 0, 2), (0, 1, 2), (1, 0, 4), (2, 0, 2), (1, 1, 4), (2, 1, 2), (3, 0, 4), (3, 1, 4)]
REACH = {1: 7, 2: 6, 4: 4, 8: 0}
SLOPES = [float(np.float32(2.0) ** np.float32(-8.0 * (h + 1) / NQ)) for h in range(NQ)]

MIX = 0
Q0, D0, WP0, K0 = 16, 24, 32, 40


def layer(nc, x, norm_pre_mix, w_in, w_pool, pool_scale, attn_sink, w_out, norm_post_mix,
          norm_pre_ffn, w_gate, w_up, conv_w, conv_b, w_down, norm_post_ffn,
          identity, distance, inverse_count, out):
    x_rows = x.rearrange("a (b p) d -> (a b) p d", p=P)
    out_rows = out.rearrange("a (b p) d -> (a b) p d", p=P)
    w_in_v = w_in.rearrange("l (k p) n -> p (l k) n", p=P)
    w_gate_v = w_gate.rearrange("l (k p) n -> p (l k) n", p=P)
    w_up_v = w_up.rearrange("l (k p) n -> p (l k) n", p=P)
    w_out_v = w_out.rearrange("l (k p) n -> p (l k) n", p=P)
    w_down_v = w_down.rearrange("l (k p) n -> p (l k) n", p=P)
    w_pool_v = w_pool.rearrange("l g (c p) d -> p (l g c) d", p=P)

    with ExitStack() as ctx:
        def sb(name, shape, dt=F32):
            return ctx.enter_context(nc.sbuf_tensor(name, shape, dt))

        def sem(name):
            return ctx.enter_context(nc.semaphore(name))

        raw = sb("raw", [P, RING, D])
        hi = sb("hi", [P, RING, D], F32R)
        lo = sb("lo", [P, RING, D], F32R)
        act = sb("act", [P, KT, 2 * S], F32R)
        pair = sb("pair", [P, RING, 2 * S], F32R)
        xbuf = sb("xbuf", [P, TB, D])
        late = sb("late", [P, FT, S])
        pads = sb("pads", [P, 4, PW])
        half = sb("half", [P, 2, S])
        dist = sb("dist", [P, TB, S])
        ident = sb("ident", [P, P])
        rows_a = sb("rows_a", [P, P])
        rows_b = sb("rows_b", [P, P])
        cols = sb("cols", [P, 4 * FT + 8])
        sink = sb("sink", [P, NQ])
        neg_sink = sb("neg_sink", [P, NQ])
        part = sb("part", [P, 8, 4])
        rstd = sb("rstd", [P, 8])
        expo = sb("expo", [P, 1])
        unused = sb("unused", [P, 1])
        small = sb("small", [P, 2, 6, 4])
        psum = ctx.enter_context(nc.psum_tensor("psum", [P, 8, 512], F32))

        xflat = xbuf[:, :, :].rearrange("p b d -> p (b d)")
        prob = [xflat[:, 1024 * b:1024 * (b + 1)].rearrange("p (h s) -> p h s", h=4) for b in range(2)]
        prob_t = xflat[:, 2048:3072].rearrange("p (k c) -> p k c", k=2)
        val = xflat[:, 3072:3584].rearrange("p (b c) -> p b c", b=2)
        val_t = xflat[:, 3584:4096].rearrange("p (u s) -> p u s", u=2)
        wide = lambda a, n=8: late[:, a:a + n, :].rearrange("p t s -> p (t s)")
        inv_count = late[:, MIX:MIX + 4, :]
        gain_row = late[0:1, MIX:MIX + 8, :].rearrange("p t s -> p (t s)")
        normed_0 = [wide(Q0), wide(D0)]
        conv_row = pads[:, 1, 0:S]
        CW0, CW1, PS, CW2, CB = 0, FT, 2 * FT, 2 * FT + 8, 3 * FT + 8

        raw_landed = [sem(f"raw_landed_{s}") for s in range(RING)]
        x_landed = [sem(f"x_landed_{k}") for k in range(TB * NC)]
        gain_landed = sem("gain_landed")
        gain_spread = sem("gain_spread")
        ident_landed = sem("ident_landed")
        dist_landed = sem("dist_landed")
        rows_landed = sem("rows_landed")
        sink_landed = sem("sink_landed")
        count_landed = sem("count_landed")
        w_pool_landed = sem("w_pool_landed")
        x_again_landed = sem("x_again_landed")
        gains2_landed = sem("gains2_landed")
        gain3_landed = sem("gain3_landed")
        stored = sem("stored")
        hi_ready = sem("hi_ready")
        lo_ready = sem("lo_ready")
        unit_done = sem("unit_done")
        pair_hi = sem("pair_hi")
        pair_lo = sem("pair_lo")
        half_ready = sem("half_ready")
        result_ready = sem("result_ready")
        y_done = sem("y_done")
        squares = sem("squares")
        rms_ready = sem("rms_ready")
        rms_step = sem("rms_step")
        consts_set = sem("consts_set")
        normed = sem("normed")
        turned = sem("turned")
        act_hi = sem("act_hi")
        act_lo = sem("act_lo")
        val_turned = sem("val_turned")
        val_ready = sem("val_ready")
        sink_ready = sem("sink_ready")
        pads_zero = sem("pads_zero")
        scores_done = sem("scores_done")
        logits_ready = sem("logits_ready")
        max_step = sem("max_step")
        bias_ready = sem("bias_ready")
        exps_ready = sem("exps_ready")
        sum_step = sem("sum_step")
        prob_ready = sem("prob_ready")
        prob_turned = sem("prob_turned")
        prob_t_ready = sem("prob_t_ready")
        heads_done = sem("heads_done")
        heads_ready = sem("heads_ready")
        gained = sem("gained")
        scaled = sem("scaled")
        pool_step = sem("pool_step")
        diff_ready = sem("diff_ready")
        pooled = sem("pooled")
        pooled_ready = sem("pooled_ready")
        resid = sem("resid")
        conv_step = sem("conv_step")
        conv_ready = sem("conv_ready")
        gelu_ready = sem("gelu_ready")
        hidden_ready = sem("hidden_ready")

        block = ctx.enter_context(nc.Block())

        @block.sync
        def _(sp):
            def load(n, c, src):
                if not isinstance(n, int) or n >= RING:
                    sp.wait_ge(lo_ready, n - RING + 1)
                dst = raw[:, c, :]
                if len(src.shape) == 3:
                    dst = dst.rearrange("p (k n) -> p k n", k=KT)
                sp.dma_start(dst, src).then_inc(raw_landed[c], 16)

            def in_columns(first):
                return w_in_v[:, :, first:first + P]

            def spread(a, gain, landed):
                sp.dma_start(wide(a), gain.partition_broadcast(P).rearrange("p l d -> p (l d)")).then_inc(landed, 16)

            firsts = (IN_W - 2 * KV_W, IN_W - 2 * KV_W + P, IN_W - KV_W, IN_W - KV_W + P)
            sp.dma_start(gain_row, norm_pre_mix).then_inc(gain_landed, 16)
            for b in range(TB):
                for h in range(NC):
                    sp.dma_start(xbuf[:, b, h * CW:(h + 1) * CW], x_rows[b][:, h * CW:(h + 1) * CW]).then_inc(x_landed[NC * b + h], 16)
            for c in range(RING):
                load(c, c, in_columns(firsts[c]))
            with sp.Fori(0, 2) as i:
                for c in range(RING):
                    load(i * RING + (U_Q + c), c, w_in_v[:, :, bass.ds(i * (RING * P) + (POOL_W + c * P), P)])
            sp.wait_ge(normed, NC * TB)
            sp.dma_start(late[:, WP0:WP0 + 8, :], w_pool_v).then_inc(w_pool_landed, 16)
            for m in range(8):
                load(U_POOL + m, m % RING, in_columns((7 - m) * P))
            for r in range(KT):
                if r == 6:
                    sp.wait_ge(heads_done, 8)
                    for b in range(TB):
                        sp.dma_start(xbuf[:, b, :], x_rows[b]).then_inc(x_again_landed, 16)
                    sp.wait_ge(pooled, 4)
                    spread(Q0, norm_post_mix, gains2_landed)
                    spread(D0, norm_pre_ffn, gains2_landed)
                load(U_OUT + r, r % RING, w_out_v[:, (r + 8) % KT, :])
            with sp.Fori(0, FT // 2) as i:
                for c in range(RING):
                    w = (w_gate_v, w_up_v)[c % 2]
                    load(i * RING + (U_FFN + c), c, w[:, :, bass.ds(i * (2 * P) + (c // 2) * P, P)])
            with sp.Fori(0, FT // RING - 1) as i:
                for c in range(RING):
                    load(i * RING + (U_DOWN + c), c, w_down_v[:, i * RING + c, :])
            sp.wait_ge(pair_lo, KT + 24)
            spread(16, norm_post_ffn, gain3_landed)
            for c in range(RING):
                load(UNITS - RING + c, c, w_down_v[:, FT - RING + c, :])
            for k in range(2 * LC):
                b, h = k // LC, k % LC
                sp.wait_ge(resid, 2 * NC + k + 1)
                sp.dma_start(out_rows[b][:, h * 512:(h + 1) * 512], xbuf[:, b, h * 512:(h + 1) * 512]).then_inc(stored, 16)
            sp.wait_ge(stored, 16 * 2 * LC)

        @block.tensor
        def _(pe):
            def turn(norm, b, source):
                for kt in range(KT):
                    if kt % 8 == 0:
                        pe.wait_ge(normed, NC * (TB * norm + b) + kt // 8 + 1)
                    mm = nc.tensor.transpose(psum[:, 4 * b + kt // 4, (kt % 4) * P:(kt % 4 + 1) * P],
                                             source[:, kt * P:(kt + 1) * P], ident[:, :])
                    if kt % 4 == 3:
                        mm.then_inc(turned, 1)

            def high_part(n, c, norm, b):
                pe.wait_ge(hi_ready, n + c + 1)
                for kt in range(KT):
                    if c == 0 and kt % 4 == 0:
                        pe.wait_ge(act_lo, 8 * norm + 4 * b + kt // 4 + 1)
                    a, o = (v.rearrange("p (h b s) -> p h b s", h=2, b=TB)[:, :, b, :] for v in (act[:, kt, :], psum[:, c, :]))
                    nc.tensor.matmul(o, hi[:, c, kt * P:(kt + 1) * P], a, start=(b == 0 and kt == 0),
                                     stop=(b == 0 and kt == KT - 1), skip_group_check=True)

            def low_part(n, c):
                pe.wait_ge(lo_ready, n + c + 1)
                for kt in range(KT):
                    mm = nc.tensor.matmul(psum[:, c, 0:S], lo[:, c, kt * P:(kt + 1) * P], act[:, kt, 0:S], start=False,
                                          stop=(kt == KT - 1), skip_group_check=True)
                mm.then_inc(unit_done, 1)

            def column_unit(n, c, bank, free_after):
                pe.wait_ge(lo_ready, n + 1)
                pe.wait_ge(result_ready, free_after)
                for kt in range(KT):
                    high = (hi[:, c, kt * P:(kt + 1) * P], act[:, kt, :], psum[:, bank, :])
                    low = (lo[:, c, kt * P:(kt + 1) * P], act[:, kt, 0:S], psum[:, bank, 0:S])
                    last = kt == KT - 1
                    for k, (w, a, o) in enumerate((low, high) if last else (high, low)):
                        mm = nc.tensor.matmul(o, w, a, start=(kt == 0 and k == 0), stop=(last and k == 1))
                mm.then_inc(unit_done, 1)

            def rows_of_block(c, b, bank, start, stop):
                a_hi, a_lo = (pair[:, c, k * S + b * P:k * S + (b + 1) * P] for k in range(2))

                def product(j, a, w, first=False, last=False):
                    return nc.tensor.matmul(psum[:, bank + j, :], a, w[:, c, j * 512:(j + 1) * 512],
                                            start=start and first, stop=last)

                if not stop:
                    for j in range(4):
                        product(j, a_hi, hi, first=True)
                        product(j, a_hi, lo)
                    return [product(j, a_lo, hi) for j in range(4)][-1]
                for j in range(4):
                    product(j, a_hi, hi)
                    product(j, a_hi, lo)
                    mm = product(j, a_lo, hi, last=True)
                    if (b, j) != (TB - 1, 3):
                        mm.then_inc(y_done, 1)
                return mm

            def row_unit(n, c, pairs, start, banks, wait_between=lambda: None):
                pe.wait_ge(lo_ready, n + 1)
                pe.wait_ge(pair_lo, pairs)
                order = (0, 1) if banks[0] == 4 else (1, 0)
                rows_of_block(c, order[0], banks[order[0]], start, False)
                wait_between()
                rows_of_block(c, order[1], banks[order[1]], start, False).then_inc(unit_done, 1)

            def last_row_units(n, pairs, banks):
                for b in range(TB):
                    for c in range(RING):
                        if b == 0:
                            pe.wait_ge(lo_ready, n + c + 1)
                            pe.wait_ge(pair_lo, pairs + c + 1)
                        mm = rows_of_block(c, b, banks[b], False, c == RING - 1)
                        if b == TB - 1:
                            mm.then_inc(unit_done, 1)

            def scores(m):
                if m >= 1:
                    pe.wait_ge(logits_ready, m)
                j, qb = m // 2, m % 2
                for t in range(2):
                    for e in range(2):
                        r = slice(64 * e, 64 * e + 64)
                        mm = nc.tensor.matmul(psum[:, 4 + e, t * S:(t + 1) * S],
                                              late[r, Q0 + 2 * j + t, qb * P:(qb + 1) * P],
                                              late[r, K0 + j, :], start=True, stop=True)
                mm.then_inc(scores_done, 1)

            def turn_probs(m):
                pe.wait_ge(prob_ready, m + 1)
                if m >= 1:
                    pe.wait_ge(prob_t_ready, m)
                for kb in range(2):
                    for hh in range(4):
                        mm = nc.tensor.transpose(psum[:, 6 + kb, hh * P:(hh + 1) * P],
                                                 prob[m % 2][:, hh, kb * P:(kb + 1) * P], ident[:, :])
                mm.then_inc(prob_turned, 1)

            def heads(m):
                pe.wait_ge(prob_t_ready, m + 1)
                if m >= 2:
                    pe.wait_ge(heads_ready, m - 1)
                j = m // 2
                for e in range(2):
                    for kb in range(2):
                        rhs = prob_t[:, kb, :].rearrange("p (t e q) -> p t e q", t=2, e=2)[:, :, e, :]
                        mm = nc.tensor.matmul(psum[64 * e:64 * e + 64, 2 + m % 2, 0:S],
                                              val[:, kb, j * HD:(j + 1) * HD], rhs,
                                              start=(kb == 0), stop=(kb == 1))
                mm.then_inc(heads_done, 1)

            pe.wait_ge(ident_landed, 16)
            for b in range(TB):
                turn(0, b, normed_0[b])
            for c in range(RING + 1):
                if c < RING:
                    for b in range(TB):
                        high_part(0, c, 0, b)
                if c > 0:
                    low_part(0, c - 1)
            with pe.Fori(0, 2) as i:
                for c in range(RING):
                    column_unit(i * RING + (U_Q + c), c, c, i * RING + (U_Q + c - RING + 1))
            pe.wait_ge(result_ready, U_Q)
            for tb in range(TB):
                for u in range(2):
                    nc.tensor.transpose(psum[:, 6, (tb * 2 + u) * P:(tb * 2 + u + 1) * P],
                                        val_t[:, u, tb * P:(tb + 1) * P], ident[:, :])
            pe.wait_ge(rows_landed, 16 * 5)
            nc.tensor.transpose(psum[:, 7, 0:2 * FT + 8], rows_a[0:2 * FT + 8, :], ident[0:2 * FT + 8, 0:2 * FT + 8])
            nc.tensor.transpose(psum[:, 7, 2 * FT + 8:4 * FT + 8], rows_b[0:2 * FT, :],
                                ident[0:2 * FT, 0:2 * FT]).then_inc(val_turned, 1)
            for m in range(8):
                if m == 0:
                    pe.wait_ge(result_ready, U_Q + 2)
                scores(m)
                n = U_POOL + m
                column_unit(n, n % RING, n % 2, n - 3 if m < 2 else n - 1)
                if m >= 2:
                    heads(m - 2)
                if m == 1:
                    pe.wait_ge(val_ready, 2)
                if m >= 1:
                    turn_probs(m - 1)
            def pool_products(g):
                pe.wait_ge(diff_ready, 8 - 2 * g)
                for mt in range(2):
                    for kc in range(2):
                        mm = nc.tensor.matmul(psum[:, (0, 1, 4, 5)[g], mt * S:(mt + 1) * S],
                                              late[:, WP0 + 2 * g + kc, mt * P:(mt + 1) * P],
                                              late[:, D0 + 2 * g + kc, :], start=(kc == 0), stop=(kc == 1))
                mm.then_inc(pooled, 1)

            pe.wait_ge(w_pool_landed, 16)
            pe.wait_ge(logits_ready, 8)
            pool_products(3)
            heads(6)
            pool_products(2)
            pe.wait_ge(result_ready, U_OUT)
            pool_products(1)
            turn_probs(7)
            pool_products(0)
            heads(7)

            def banks_0_to_3_free():
                pe.wait_ge(pooled_ready, 8)
                pe.wait_ge(heads_ready, 8)

            pe.wait_ge(pooled_ready, 4)
            for r in range(KT - RING):
                row_unit(U_OUT + r, r % RING, r + 1, r == 0, (0, 4), banks_0_to_3_free if r == 0 else lambda: None)
            last_row_units(U_FFN - RING, KT - RING, (0, 4))
            pe.wait_ge(scaled, 4)

            turn(1, 0, wide(WP0))
            for c in range(RING):
                high_part(U_FFN, c, 1, 0)
            turn(1, 1, wide(MIX))
            for c in range(RING):
                high_part(U_FFN, c, 1, 1)
                low_part(U_FFN, c)
            with pe.Fori(1, FT // 2) as i:
                for c in range(RING):
                    column_unit(i * RING + (U_FFN + c), c, c, i * RING + (U_OUT + c - RING + 1))

            for c in range(RING):
                row_unit(U_DOWN + c, c, KT + c + 1, c == 0, (4, 0),
                         (lambda: pe.wait_ge(result_ready, U_OUT + 2 * FT)) if c == 0 else lambda: None)
            with pe.Fori(1, FT // RING - 1) as i:
                for c in range(RING):
                    row_unit(i * RING + (U_DOWN + c), c, i * RING + (KT + c + 1), False, (4, 0))
            last_row_units(UNITS - RING, KT + FT - RING, (4, 0))

        @block.scalar
        def _(sc):
            def split(n, c):
                if n >= RING:
                    sc.wait_ge(unit_done, n - RING + 1)
                sc.wait_ge(raw_landed[c], (n // RING + 1) * 16)
                nc.scalar.copy(hi[:, c, :], raw[:, c, :]).then_inc(hi_ready, 1)

            def split_looped(i, first, c):
                sc.wait_ge(unit_done, i * RING + (first + c - RING + 1))
                sc.wait_ge(raw_landed[c], i * 16 + (first // RING + 1) * 16)
                nc.scalar.copy(hi[:, c, :], raw[:, c, :]).then_inc(hi_ready, 1)

            def split_pair(tile, c):
                nc.scalar.copy(pair[:, c, 0:S], late[:, tile, :]).then_inc(pair_hi, 1)

            def half_out(n, c, bank, scale=1.0):
                sc.wait_ge(unit_done, n + 1)
                nc.scalar.activation(half[:, c % 2, :], psum[:, bank, S:2 * S], ACT.Copy, scale=scale).then_inc(half_ready, 1)

            def act_high(norm, b):
                for k in range(4):
                    sc.wait_ge(turned, 8 * norm + 4 * b + k + 1)
                    nc.scalar.copy(act[:, 4 * k:4 * k + 4, b * P:(b + 1) * P],
                                   psum[:, 4 * b + k, :].rearrange("p (t s) -> p t s", t=4)).then_inc(act_hi, 1)

            def squares_of(norm, b, wait, source):
                first, n = squares_before(norm, b)
                for k in range(n):
                    wait(k)
                    if first + k >= 2:
                        sc.wait_ge(squares, first + k - 1)
                    w = D // n
                    nc.scalar.activation(scratch[(first + k) % 2][:, 0:w], source(k, w), ACT.Square,
                                         accum_out=part[:, TB * norm + b, k:k + 1]).then_inc(squares, 1)

            scratch = [wide(MIX + 8 + 4 * k, 4) for k in range(2)]

            def squares_of_x(norm, b):
                squares_of(norm, b, lambda k: sc.wait_ge(*((x_landed[NC * b + k], 16) if norm == 0 else (resid, NC * b + k + 1))),
                           lambda k, w: xbuf[:, b, k * w:(k + 1) * w])

            def squares_of_y(norm, b, bank, product, last_unit):
                squares_of(norm, b, lambda k: sc.wait_ge(*((unit_done, last_unit + 1) if (b, k) == (TB - 1, 3)
                                                           else (y_done, 7 * product + 4 * b + k + 1))),
                           lambda k, w: psum[:, bank + k, :])

            sc.dma_start(ident[:, :], identity).then_inc(ident_landed, 16)
            squares_of_x(0, 0)
            squares_of_x(0, 1)
            act_high(0, 0)
            split(0, 0)
            act_high(0, 1)
            for c in range(1, RING):
                split(c, c)
            for k, (dst, a, src) in enumerate(((rows_a, 0, conv_w[0, 0]), (rows_a, FT, conv_w[0, 1]), (rows_a, 2 * FT, pool_scale[0]),
                                               (rows_b, 0, conv_w[0, 2]), (rows_b, FT, conv_b[0]))):
                t = src.shape[0] // P
                sc.dma_start(dst[a:a + t, :], src.rearrange("(t p) -> t p", p=P)).then_inc(rows_landed, 16)
            sc.dma_start(sink[:, :], attn_sink.partition_broadcast(P).rearrange("p l h -> p (l h)")).then_inc(sink_landed, 16)
            sc.dma_start(dist[:, :, :], distance.rearrange("b p s -> p b s")).then_inc(dist_landed, 16)
            sc.wait_ge(squares, 4)
            sc.dma_start(inv_count, inverse_count.partition_broadcast(P)).then_inc(count_landed, 16)

            for n in range(U_Q):
                if n >= 2:
                    sc.wait_ge(result_ready, n - 1)
                half_out(n, n, n)
                split(n + RING, n % RING)
            with sc.Fori(0, 2) as i:
                for c in range(RING):
                    sc.wait_ge(result_ready, i * RING + (U_Q + c - 1))
                    half_out(i * RING + (U_Q + c), c, c, HD ** -0.5)
                    split_looped(i, 2 * RING, c)
            sc.wait_ge(val_turned, 1)
            nc.scalar.copy(val, psum[:, 6, :].rearrange("p (b c) -> p b c", b=2)).then_inc(val_ready, 1)
            nc.scalar.copy(cols[:, :], psum[:, 7, 0:4 * FT + 8]).then_inc(val_ready, 1)

            def exps(m):
                sc.wait_ge(bias_ready, m + 1)
                s = small[:, m % 2]
                for hh in range(4):
                    h = prob[m % 2][:, hh, :]
                    nc.scalar.activation(h, h, ACT.Exp, bias=s[:, 1, hh:hh + 1], accum_out=s[:, 3, hh:hh + 1])
                nc.scalar.activation(s[:, 4, :], s[:, 2, :], ACT.Exp).then_inc(exps_ready, 1)

            def probs_out(m):
                sc.wait_ge(prob_turned, m + 1)
                if m >= 1:
                    sc.wait_ge(heads_done, m)
                nc.scalar.copy(prob_t, psum[:, 6:8, :]).then_inc(prob_t_ready, 1)

            def heads_out(m):
                sc.wait_ge(heads_done, m + 1)
                j, qb = m // 2, m % 2
                nc.scalar.copy(late[:, MIX + 8 + 2 * j:MIX + 10 + 2 * j, qb * P:(qb + 1) * P],
                               psum[:, 2 + m % 2, 0:S].rearrange("p (t q) -> p t q", t=2)).then_inc(heads_ready, 1)

            for m in range(8):
                n = U_POOL + m
                exps(m)
                sc.wait_ge(result_ready, n - 1)
                half_out(n, n, n % 2)
                if m >= 2:
                    heads_out(m - 2)
                if m >= 1:
                    probs_out(m - 1)
                split(n + RING, n % RING)
                if m >= RING:
                    r = m - RING
                    sc.wait_ge(heads_ready, 2 * (r // 2) + 2)
                    split_pair(MIX + 8 + r, r)
            def pooled_out(g):
                sc.wait_ge(pooled, 4 - g)
                for t in (2 * g, 2 * g + 1):
                    nc.scalar.activation(late[:, MIX + t, :], psum[:, (0, 1, 4, 5)[g], (t % 2) * S:(t % 2 + 1) * S], ACT.Copy,
                                         scale=cols[:, PS + t:PS + t + 1]).then_inc(pooled_ready, 1)

            sc.wait_ge(val_ready, 2)
            sc.wait_ge(diff_ready, 8)
            pooled_out(3)
            heads_out(6)
            pooled_out(2)
            pooled_out(1)
            probs_out(7)
            pooled_out(0)
            heads_out(7)

            nc.scalar.activation(unused[:, :], cols[:, CB:CB + 1], ACT.Gelu_apprx_tanh)

            for r in range(KT - RING):
                split(U_OUT + r + RING, r % RING)
                if r == 0:
                    sc.wait_ge(heads_ready, 8)
                    sc.wait_ge(pooled_ready, 8)
                split_pair(MIX + (r + RING + 8) % KT, r % RING)

            sc.wait_ge(pair_lo, KT)
            squares_of_y(1, 0, 0, 0, U_FFN - 1)
            squares_of_x(2, 0)
            split(U_FFN, 0)
            split(U_FFN + 1, 1)
            squares_of_y(1, 1, 4, 0, U_FFN - 1)
            act_high(1, 0)
            split(U_FFN + 2, 2)
            split(U_FFN + 3, 3)
            squares_of_x(2, 1)
            act_high(1, 1)

            def ffn_tile(i, ct):
                c = 2 * ct
                sc.wait_ge(result_ready, i * RING + (U_OUT + c - 1))
                half_out(i * RING + (U_FFN + c), c, c)
                split_looped(i, U_FFN + RING, c)
                sc.wait_ge(conv_ready, i * 2 + (ct + 1))
                nc.scalar.activation(conv_row, conv_row, ACT.Gelu_apprx_tanh,
                                     bias=cols[:, bass.ds(i * 2 + (CB + ct), 1)]).then_inc(gelu_ready, 1)
                sc.wait_ge(result_ready, i * RING + (U_OUT + c))
                half_out(i * RING + (U_FFN + c + 1), c + 1, c + 1)
                split_looped(i, U_FFN + RING, c + 1)

            with sc.Fori(0, FT // 2 - 1) as i:
                for ct in range(2):
                    ffn_tile(i, ct)
            for c in range(RING):
                sc.wait_ge(hidden_ready, c + 1)
                split_pair(c, c)
            for ct in range(2):
                ffn_tile(FT // 2 - 1, ct)

            with sc.Fori(0, FT // RING - 1) as i:
                for c in range(RING):
                    split_looped(i, U_DOWN + RING, c)
                    if c == 0:
                        sc.wait_ge(hidden_ready, FT)
                    split_pair(i * RING + (RING + c), c)

            sc.wait_ge(pair_lo, KT + 16)
            squares_of_y(3, 0, 4, 1, UNITS - 1)
            squares_of_y(3, 1, 0, 1, UNITS - 1)

        @block.vector
        def _(ve):
            def split(n, c):
                ve.wait_ge(hi_ready, n + 1)
                nc.vector.tensor_tensor(lo[:, c, :], raw[:, c, :], hi[:, c, :].bitcast(F32), ALU.subtract).then_inc(lo_ready, 1)

            def split_pair(tile, c, count):
                ve.wait_ge(pair_hi, count)
                nc.vector.tensor_tensor(pair[:, c, S:2 * S], late[:, tile, :], pair[:, c, 0:S].bitcast(F32),
                                        ALU.subtract).then_inc(pair_lo, 1)

            def act_low(norm, b):
                for k in range(4):
                    at = act[:, 4 * k:4 * k + 4, :]
                    ve.wait_ge(act_hi, 8 * norm + 4 * b + k + 1)
                    nc.vector.tensor_tensor(at[:, :, S + b * P:S + (b + 1) * P],
                                            psum[:, 4 * b + k, :].rearrange("p (t s) -> p t s", t=4),
                                            at[:, :, b * P:(b + 1) * P].bitcast(F32), ALU.subtract).then_inc(act_lo, 1)

            def gain_rows(b, to, gain, ready):
                for h in range(NC):
                    w = slice(h * CW, (h + 1) * CW)
                    ready(h)
                    nc.vector.tensor_tensor(to[:, w], xbuf[:, b, w], gain[:, w], ALU.mult).then_inc(gained, 1)

            def norm_rows(norm, slot, b, to, before):
                ve.wait_ge(rms_ready, slot)
                for h in range(NC):
                    w = slice(h * CW, (h + 1) * CW)
                    ve.wait_ge(gained, before + h + 1)
                    nc.vector.tensor_scalar(to[:, w], to[:, w], rstd[:, TB * norm + b:TB * norm + b + 1], None,
                                            ALU.mult).then_inc(normed, 1)

            nc.vector.memset(expo[:, :], -0.5).then_inc(consts_set, 1)
            nc.vector.memset(pads[:, :, :], 0.0).then_inc(pads_zero, 1)
            ve.wait_ge(gain_spread, 1)
            gain_rows(0, normed_0[0], wide(WP0), lambda h: ve.wait_ge(x_landed[h], 16))
            norm_rows(0, 1, 0, normed_0[0], 0)
            gain_rows(1, normed_0[1], wide(WP0), lambda h: ve.wait_ge(x_landed[NC + h], 16))
            norm_rows(0, 2, 1, normed_0[1], NC)
            act_low(0, 0)
            act_low(0, 1)
            for c in range(RING):
                split(c, c)
            ve.wait_ge(sink_landed, 16)
            nc.vector.tensor_scalar(neg_sink[:, :], sink[:, :], -1.0, None, ALU.mult).then_inc(sink_ready, 1)

            for n in range(2):
                ve.wait_ge(half_ready, n + 1)
                for e in range(2):
                    for to in range(2):
                        s, r = slice(64 * e, 64 * e + 64), slice(64 * to, 64 * to + 64)
                        op = nc.vector.tensor_tensor(late[r, K0 + 2 * n + e, :], psum[s, n, 0:S], half[s, n, :], ALU.add)
                op.then_inc(result_ready, 1)
                if n:
                    split(n + 3, (n + 3) % RING)
            for n in range(2, 4):
                ve.wait_ge(half_ready, n + 1)
                nc.vector.tensor_tensor(val_t[:, n - 2, :], psum[:, n, 0:S], half[:, n % 2, :], ALU.add).then_inc(result_ready, 1)
                split(n + 3, (n + 3) % RING)
            with ve.Fori(0, 2) as i:
                for c in range(RING):
                    ve.wait_ge(half_ready, i * RING + (U_Q + c + 1))
                    nc.vector.scalar_tensor_tensor(out=late[:, i * RING + (Q0 + c), :], in0=psum[:, c, 0:S], scalar=HD ** -0.5,
                                                   in1=half[:, c % 2, :], op0=ALU.mult, op1=ALU.add).then_inc(result_ready, 1)
                    split(i * RING + (U_Q + c + 3), (c + 3) % RING)

            ve.wait_ge(sink_ready, 1)
            ve.wait_ge(dist_landed, 16)
            for m in range(8):
                n, j, qb = U_POOL + m, m // 2, m % 2
                s, p = small[:, m % 2], prob[m % 2]
                ve.wait_ge(scores_done, m + 1)
                if m >= 2:
                    ve.wait_ge(prob_turned, m - 1)
                for hh in range(4):
                    op = nc.vector.scalar_tensor_tensor(out=p[:, hh, :], in0=dist[:, qb, :], scalar=-SLOPES[4 * j + hh],
                                                        in1=psum[:, 4 + hh % 2, (hh // 2) * S:(hh // 2 + 1) * S],
                                                        op0=ALU.mult, op1=ALU.add)
                op.then_inc(logits_ready, 1)
                ve.wait_ge(logits_ready, m + 1)
                nc.vector.reduce_max(s[:, 0, :], p, AX_X).then_inc(max_step, 1)
                ve.wait_ge(max_step, 2 * m + 1)
                nc.vector.scalar_tensor_tensor(out=s[:, 1, :], in0=s[:, 0, :], scalar=-1.0, in1=neg_sink[:, 4 * j:4 * j + 4],
                                               op0=ALU.mult, op1=ALU.min).then_inc(max_step, 1)
                ve.wait_ge(max_step, 2 * m + 2)
                nc.vector.tensor_tensor(s[:, 2, :], s[:, 1, :], sink[:, 4 * j:4 * j + 4], ALU.add).then_inc(bias_ready, 1)
                split(n + 3, (n + 3) % RING)
                if m > RING:
                    r = m - RING - 1
                    split_pair(MIX + 8 + r, r, r + 1)
                ve.wait_ge(exps_ready, m + 1)
                nc.vector.tensor_tensor(s[:, 3, :], s[:, 3, :], s[:, 4, :], ALU.add).then_inc(sum_step, 1)
                ve.wait_ge(sum_step, 2 * m + 1)
                nc.vector.reciprocal(s[:, 5, :], s[:, 3, :]).then_inc(sum_step, 1)
                ve.wait_ge(sum_step, 2 * m + 2)
                for hh in range(4):
                    op = nc.vector.tensor_scalar(p[:, hh, :], p[:, hh, :], s[:, 5, hh:hh + 1], None, ALU.mult)
                op.then_inc(prob_ready, 1)
                ve.wait_ge(half_ready, n + 1)
                if m >= 2:
                    ve.wait_ge(diff_ready, m - 1)
                nc.vector.tensor_tensor(pads[:, m % 2, PAD:PAD + S], psum[:, n % 2, 0:S], half[:, n % 2, :],
                                        ALU.add).then_inc(result_ready, 1)
            split_pair(MIX + 11, 3, 4)
            for r in range(KT - 3):
                split(U_OUT + r + 3, (r + 3) % RING)
                if r + RING < KT:
                    split_pair(MIX + (r + RING + 8) % KT, r % RING, r + RING + 1)

            def gain_y(b, bank, product, gain, temp):
                first = squares_before(2 * product + 1, b)[0]
                for j in range(4):
                    at = slice(j * 512, (j + 1) * 512)
                    ve.wait_ge(squares, first + j + 1)
                    nc.vector.tensor_tensor(temp[:, at], psum[:, bank + j, :], gain[:, at], ALU.mult).then_inc(scaled, 1)

            def residual(norm, slot, b, temp, before, chunks):
                ve.wait_ge(rms_ready, slot)
                ve.wait_ge(scaled, before + 4)
                w = D // chunks
                for h in range(chunks):
                    at = slice(h * w, (h + 1) * w)
                    nc.vector.scalar_tensor_tensor(out=xbuf[:, b, at], in0=temp[:, at], scalar=rstd[:, TB * norm + b:TB * norm + b + 1],
                                                   in1=xbuf[:, b, at], op0=ALU.mult, op1=ALU.add).then_inc(resid, 1)

            ve.wait_ge(x_again_landed, 16 * TB)
            ve.wait_ge(gains2_landed, 32)
            temps = (wide(WP0), wide(MIX))

            def gain_new_x(b):
                gain_rows(b, temps[b], wide(D0), lambda h: ve.wait_ge(resid, NC * b + h + 1))

            gain_y(0, 0, 0, wide(Q0), temps[0])
            residual(1, 3, 0, temps[0], 0, NC)
            gain_new_x(0)
            norm_rows(2, 4, 0, temps[0], 2 * NC)
            split(U_FFN, 0)
            gain_y(1, 4, 0, wide(Q0), temps[1])
            act_low(1, 0)
            residual(1, 5, 1, temps[1], 4, NC)
            gain_new_x(1)
            norm_rows(2, 6, 1, temps[1], 3 * NC)
            act_low(1, 1)
            split(U_FFN + 1, 1)
            split(U_FFN + 2, 2)
            split(U_FFN + 3, 3)

            gate, up = pads[:, 0, PAD - 1:PAD + S + 1], pads[:, 2, 0:S]
            ve.wait_ge(diff_ready, 8)

            def ffn_tile(i, ct, ahead=True):
                c = 2 * ct
                ve.wait_ge(half_ready, i * RING + (U_OUT + c + 1))
                nc.vector.tensor_tensor(gate[:, 1:1 + S], psum[:, c, 0:S], half[:, 0, :], ALU.add).then_inc(result_ready, 1)
                ve.wait_ge(result_ready, i * RING + (U_OUT + c + 1))
                nc.vector.tensor_scalar(conv_row, gate[:, 0:S], cols[:, bass.ds(i * 2 + (CW0 + ct), 1)], None, ALU.mult).then_inc(conv_step, 1)
                ve.wait_ge(conv_step, i * 4 + (2 * ct + 1))
                nc.vector.scalar_tensor_tensor(out=conv_row, in0=gate[:, 1:1 + S], scalar=cols[:, bass.ds(i * 2 + (CW1 + ct), 1)],
                                               in1=conv_row, op0=ALU.mult, op1=ALU.add).then_inc(conv_step, 1)
                ve.wait_ge(conv_step, i * 4 + (2 * ct + 2))
                nc.vector.scalar_tensor_tensor(out=conv_row, in0=gate[:, 2:2 + S], scalar=cols[:, bass.ds(i * 2 + (CW2 + ct), 1)],
                                               in1=conv_row, op0=ALU.mult, op1=ALU.add).then_inc(conv_ready, 1)
                if ahead:
                    split(i * RING + (U_FFN + c + 3), (c + 3) % RING)
                ve.wait_ge(half_ready, i * RING + (U_OUT + c + 2))
                nc.vector.tensor_tensor(up, psum[:, c + 1, 0:S], half[:, 1, :], ALU.add).then_inc(result_ready, 1)
                ve.wait_ge(result_ready, i * RING + (U_OUT + c + 2))
                ve.wait_ge(gelu_ready, i * 2 + (ct + 1))
                nc.vector.tensor_tensor(late[:, i * 2 + ct, :], up, conv_row, ALU.mult).then_inc(hidden_ready, 1)
                split(i * RING + (U_FFN + c + 4), c)

            for ct in range(2):
                ffn_tile(0, ct, ct > 0)
            with ve.Fori(1, FT // 2 - 1) as i:
                for ct in range(2):
                    ffn_tile(i, ct)
            for c in range(RING):
                split_pair(c, c, KT + c + 1)
            for ct in range(2):
                ffn_tile(FT // 2 - 1, ct)

            with ve.Fori(0, FT // RING - 1) as i:
                for c in range(RING):
                    split(i * RING + (U_DOWN + 3 + c), (c + 3) % RING)
                    split_pair(i * RING + (RING + c), c, i * RING + (KT + RING + c + 1))
            split(UNITS - 1, RING - 1)

            ve.wait_ge(gain3_landed, 16)
            for b in range(TB):
                temp = wide(24 + 8 * b)
                gain_y(b, 4 - 4 * b, 1, wide(16), temp)
                residual(3, 7 + b, b, temp, 8 + 4 * b, LC)

        @block.gpsimd
        def _(gp):
            tiny = [0]

            def rms(slot):
                norm, b, n = SQUARES[slot]
                before = sum(x[2] for x in SQUARES[:slot])
                k = TB * norm + b
                total = part[:, k, 0:1]

                def stepped(op):
                    op.then_inc(rms_step, 1)
                    tiny[0] += 1
                    gp.wait_ge(rms_step, tiny[0])

                gp.wait_ge(squares, before + 1)
                for j in range(1, n - 1):
                    gp.wait_ge(squares, before + j + 1)
                    stepped(nc.gpsimd.tensor_tensor(total, total, part[:, k, j:j + 1], ALU.add))
                stepped(nc.gpsimd.tensor_scalar(total, total, 1.0 / D, EPS, ALU.mult, ALU.add))
                gp.wait_ge(squares, before + n)
                stepped(nc.gpsimd.tensor_scalar(total, part[:, k, n - 1:n], 1.0 / D, total, ALU.mult, ALU.add))
                nc.gpsimd.tensor_tensor(rstd[:, k:k + 1], total, expo[:, :], ALU.pow).then_inc(rms_ready, 1)

            gp.wait_ge(gain_landed, 16)
            nc.gpsimd.partition_broadcast(wide(WP0), gain_row, P).then_inc(gain_spread, 1)
            gp.wait_ge(consts_set, 1)
            for slot in range(2):
                rms(slot)
            gp.wait_ge(pads_zero, 1)
            gp.wait_ge(count_landed, 16)
            step = 0

            for m in range(8):
                c = 7 - m
                g = c // 2
                gp.wait_ge(result_ready, U_POOL + m + 1)
                source = pads[:, m % 2, :]
                now = source
                w = 1
                while w < WINDOWS[g]:
                    back, ahead = (1, 0) if w == 1 else (w // 2, w // 2)
                    a, b = PAD - REACH[w], PAD + S + REACH[w]
                    to = pads[:, 2 + (w.bit_length() % 2), :]
                    nc.gpsimd.tensor_tensor(to[:, a:b], now[:, a - back:b - back], now[:, a + ahead:b + ahead],
                                            ALU.add).then_inc(pool_step, 1)
                    step += 1
                    gp.wait_ge(pool_step, step)
                    now, w = to, 2 * w
                other = pads[:, 2 + (w.bit_length() % 2), 0:S]
                nc.gpsimd.tensor_tensor(other, now[:, PAD:PAD + S], inv_count[:, g, :], ALU.mult).then_inc(pool_step, 1)
                step += 1
                gp.wait_ge(pool_step, step)
                nc.gpsimd.tensor_tensor(late[:, D0 + c, :], other, source[:, PAD:PAD + S], ALU.subtract).then_inc(diff_ready, 1)
                gp.wait_ge(diff_ready, m + 1)
            for slot in range(2, len(SQUARES)):
                rms(slot)


def squares_before(norm, b):
    k = [x[:2] for x in SQUARES].index((norm, b))
    return sum(x[2] for x in SQUARES[:k]), SQUARES[k][2]


NAMES = ["x", "norm_pre_mix", "w_in", "w_pool", "pool_scale", "attn_sink", "w_out", "norm_post_mix", "norm_pre_ffn",
         "w_gate", "w_up", "conv_w", "conv_b", "w_down", "norm_post_ffn"]


def shape_constants():
    q, k = np.arange(S)[:, None], np.arange(S)[None, :]
    d = np.abs(q - k).astype(np.float32)
    d = np.where(d <= WINDOW, d, np.float32(FAR)).astype(np.float32).reshape(TB, P, S)
    t = np.arange(S)
    count = [np.clip(t + w // 2, 0, S) - np.clip(t - w // 2, 0, S) for w in WINDOWS]
    inv = (np.float32(1) / np.stack(count).astype(np.float32)).astype(np.float32)
    return {"identity": np.eye(P, dtype=np.float32), "distance": d, "inverse_count": inv}


def kernel(**inputs):
    import concourse.bacc as bacc
    from concourse.bass_utils import run_bass_kernel_spmd

    nc = bacc.Bacc("TRN2", target_bir_lowering=False, num_devices=1)
    arrays, args = {}, []
    for name, a in [(n, inputs[n]) for n in NAMES] + list(shape_constants().items()):
        a = np.ascontiguousarray(a)
        arrays[f"in_{name}"] = a
        args.append(nc.dram_tensor(f"in_{name}", a.shape, mybir.dt.from_np(a.dtype), kind="ExternalInput").ap())
    args.append(nc.dram_tensor("out_y", (1, S, D), F32, kind="ExternalOutput").ap())
    layer(nc, *args)
    r = run_bass_kernel_spmd(nc, [arrays], core_ids=[0])
    return r.results[0]["out_y"]
```
